# Optimizing a Trainium2 kernel written in Bass

```python
import jax, jax.numpy as jnp
from jax import lax
import numpy as np

D_MODEL = 1024
BATCH = 1
SEQ = 512
DEPTH = 1

CHUNK = 64
Q_BLOCK = 128
EPS = 1e-6
HEAD_DIM = 64
A_HEADS = 6
A_WIDTH = A_HEADS * HEAD_DIM
IDX_HEADS = 8
IDX_DIM = 64
TOPK_MAX = 256
ALIBI_MAX = 8.0
B_HEADS = 6
B_NOPE = 64
B_ROPE = 32
B_V = 64
B_WIDTH = B_HEADS * B_V
Q_LORA = 256
KV_LORA = 128
ROPE_THETA = 10000.0
M_HEADS = 4
M_WIDTH = M_HEADS * HEAD_DIM
N_MEM = 256
D_MIX = A_WIDTH + B_WIDTH + M_WIDTH
IN_SPLITS = (A_WIDTH, A_WIDTH, A_WIDTH, IDX_HEADS * IDX_DIM, IDX_DIM, IDX_HEADS, A_WIDTH,
             Q_LORA, KV_LORA, B_ROPE, B_WIDTH,
             M_WIDTH, M_WIDTH)
D_IN = sum(IN_SPLITS)

kernel_name = "hybrid_dsa_mla_memory_gated_layer"

def rms_norm(x, g):
    xf = x.astype(jnp.float32)
    y = xf * lax.rsqrt(jnp.mean(xf * xf, axis=-1, keepdims=True) + EPS)
    return (y * g.astype(jnp.float32)).astype(x.dtype)

def rope(x, pos):
    half = x.shape[-1] // 2
    inv = 1.0 / (ROPE_THETA ** (jnp.arange(half, dtype=jnp.float32) / half))
    ang = pos.astype(jnp.float32)[:, None] * inv[None, :]
    cos = jnp.cos(ang)[None, :, None, :]
    sin = jnp.sin(ang)[None, :, None, :]
    xf = x.astype(jnp.float32)
    x1, x2 = xf[..., :half], xf[..., half:]
    return jnp.concatenate([x1 * cos - x2 * sin, x1 * sin + x2 * cos], axis=-1).astype(x.dtype)

def alibi_slopes(n):
    return 2.0 ** (-ALIBI_MAX * jnp.arange(1, n + 1, dtype=jnp.float32) / n)

def sweep_query_blocks(fn, seq):
    out = lax.map(fn, jnp.arange(seq // Q_BLOCK))
    nb, b, qb, h, d = out.shape
    return jnp.transpose(out, (1, 0, 2, 3, 4)).reshape(b, nb * qb, h, d)

def dsa_attention(q, k, v, q_idx, k_idx, w_idx, g_q, g_k, pos, topk):
    B, S, _ = q.shape
    q = rms_norm(q.reshape(B, S, A_HEADS, HEAD_DIM), g_q)
    k = rms_norm(k.reshape(B, S, A_HEADS, HEAD_DIM), g_k)
    v = v.reshape(B, S, A_HEADS, HEAD_DIM)
    q_idx = q_idx.reshape(B, S, IDX_HEADS, IDX_DIM)
    slopes = alibi_slopes(A_HEADS)
    chunk = pos // CHUNK
    scale = HEAD_DIM ** -0.5

    def block(i):
        start = i * Q_BLOCK
        qpos = lax.dynamic_slice_in_dim(pos, start, Q_BLOCK)
        qchunk = qpos // CHUNK
        qi_blk = lax.dynamic_slice_in_dim(q_idx, start, Q_BLOCK, axis=1)
        w_blk = lax.dynamic_slice_in_dim(w_idx, start, Q_BLOCK, axis=1)
        q_blk = lax.dynamic_slice_in_dim(q, start, Q_BLOCK, axis=1)
        rel = jnp.einsum('bqhd,bkd->bqhk', qi_blk, k_idx).astype(jnp.float32)
        score = jnp.einsum('bqh,bqhk->bqk', w_blk.astype(jnp.float32), jax.nn.relu(rel))
        admissible = chunk[None, :] <= qchunk[:, None]
        score = jnp.where(admissible[None], score, -jnp.inf)
        _, idx = lax.top_k(score, topk)
        valid = (idx // CHUNK) <= qchunk[None, :, None]
        k_sel = jax.vmap(lambda kb, ib: kb[ib])(k, idx)
        v_sel = jax.vmap(lambda vb, ib: vb[ib])(v, idx)
        s = jnp.einsum('bqhd,bqkhd->bhqk', q_blk, k_sel).astype(jnp.float32) * scale
        dist = jnp.abs(qpos[None, :, None] - idx).astype(jnp.float32)
        s = s - slopes[None, :, None, None] * dist[:, None]
        s = jnp.where(valid[:, None], s, -jnp.inf)
        p = jax.nn.softmax(s, axis=-1).astype(v.dtype)
        return jnp.einsum('bhqk,bqkhd->bqhd', p, v_sel)

    return sweep_query_blocks(block, S)

def mla_attention(c_q, c_kv, k_rope, w_uq, g_cq, w_ukv, g_ckv, g_q, g_k, pos):
    B, S, _ = c_q.shape
    q = (rms_norm(c_q, g_cq) @ w_uq).reshape(B, S, B_HEADS, B_NOPE + B_ROPE)
    kv = (rms_norm(c_kv, g_ckv) @ w_ukv).reshape(B, S, B_HEADS, B_NOPE + B_V)
    k_nope, v = kv[..., :B_NOPE], kv[..., B_NOPE:]
    k = jnp.concatenate(
        [k_nope, jnp.broadcast_to(k_rope[:, :, None, :], (B, S, B_HEADS, B_ROPE))], axis=-1)
    q = rms_norm(q, g_q)
    k = rms_norm(k, g_k)
    q = jnp.concatenate([q[..., :B_NOPE], rope(q[..., B_NOPE:], pos)], axis=-1)
    k = jnp.concatenate([k[..., :B_NOPE], rope(k[..., B_NOPE:], pos)], axis=-1)
    scale = (B_NOPE + B_ROPE) ** -0.5
    chunk = pos // CHUNK

    def block(i):
        start = i * Q_BLOCK
        q_blk = lax.dynamic_slice_in_dim(q, start, Q_BLOCK, axis=1)
        qchunk = lax.dynamic_slice_in_dim(chunk, start, Q_BLOCK)
        s = jnp.einsum('bqhd,bkhd->bhqk', q_blk, k).astype(jnp.float32) * scale
        s = jnp.where(chunk[None, :] <= qchunk[:, None], s, -jnp.inf)
        p = jax.nn.softmax(s, axis=-1).astype(v.dtype)
        return jnp.einsum('bhqk,bkhd->bqhd', p, v)

    return sweep_query_blocks(block, S)

def memory_attention(q, mem, g_mem, w_mk, w_mv, g_q, g_k):
    B, S, _ = q.shape
    N = mem.shape[1]
    q = rms_norm(q.reshape(B, S, M_HEADS, HEAD_DIM), g_q)
    m = rms_norm(mem, g_mem)
    k = rms_norm((m @ w_mk).reshape(B, N, M_HEADS, HEAD_DIM), g_k)
    v = (m @ w_mv).reshape(B, N, M_HEADS, HEAD_DIM)
    s = jnp.einsum('bqhd,bkhd->bhqk', q, k).astype(jnp.float32) * (HEAD_DIM ** -0.5)
    p = jax.nn.softmax(s, axis=-1).astype(v.dtype)
    return jnp.einsum('bhqk,bkhd->bqhd', p, v)

def setup_inputs(seed: int = 0) -> dict:
    key = jax.random.key(seed)
    ks = jax.random.split(key, 20)
    f32 = jnp.float32

    def w(k, shape, fan_in):
        return jax.random.normal(k, shape, f32) * (fan_in ** -0.5)

    def gain(k, shape):
        return 1.0 + 0.1 * jax.random.normal(k, shape, f32)

    return {
        "x": jax.random.normal(ks[0], (BATCH, SEQ, D_MODEL), f32),
        "mem": jax.random.normal(ks[1], (BATCH, N_MEM, D_MODEL), f32),
        "g_in": gain(ks[2], (DEPTH, D_MODEL)),
        "w_in": w(ks[3], (DEPTH, D_MODEL, D_IN), D_MODEL),
        "w_uq": w(ks[4], (DEPTH, Q_LORA, B_HEADS * (B_NOPE + B_ROPE)), Q_LORA),
        "g_cq": gain(ks[5], (DEPTH, Q_LORA)),
        "w_ukv": w(ks[6], (DEPTH, KV_LORA, B_HEADS * (B_NOPE + B_V)), KV_LORA),
        "g_ckv": gain(ks[7], (DEPTH, KV_LORA)),
        "g_qa": gain(ks[8], (DEPTH, HEAD_DIM)),
        "g_ka": gain(ks[9], (DEPTH, HEAD_DIM)),
        "g_qb": gain(ks[10], (DEPTH, B_NOPE + B_ROPE)),
        "g_kb": gain(ks[11], (DEPTH, B_NOPE + B_ROPE)),
        "g_mem": gain(ks[12], (DEPTH, D_MODEL)),
        "w_mk": w(ks[13], (DEPTH, D_MODEL, M_WIDTH), D_MODEL),
        "w_mv": w(ks[14], (DEPTH, D_MODEL, M_WIDTH), D_MODEL),
        "g_qm": gain(ks[15], (DEPTH, HEAD_DIM)),
        "g_km": gain(ks[16], (DEPTH, HEAD_DIM)),
        "w_out": w(ks[17], (DEPTH, D_MIX, D_MODEL), D_MIX),
    }

def reference(x, mem, g_in, w_in, w_uq, g_cq, w_ukv, g_ckv, g_qa, g_ka, g_qb, g_kb,
              g_mem, w_mk, w_mv, g_qm, g_km, w_out):
    B, S, _ = x.shape
    pos = jnp.arange(S, dtype=jnp.int32)
    topk = min(TOPK_MAX, S // 4)
    offsets = [int(o) for o in np.cumsum(IN_SPLITS)[:-1]]
    for l in range(DEPTH):
        h = rms_norm(x, g_in[l])
        u = h @ w_in[l]
        (q_a, k_a, v_a, q_idx, k_idx, w_idx, z_a,
         c_q, c_kv, k_rope, z_b, q_m, z_m) = jnp.split(u, offsets, axis=-1)
        y_a = dsa_attention(q_a, k_a, v_a, q_idx, k_idx, w_idx, g_qa[l], g_ka[l], pos, topk)
        y_b = mla_attention(c_q, c_kv, k_rope, w_uq[l], g_cq[l], w_ukv[l], g_ckv[l],
                            g_qb[l], g_kb[l], pos)
        y_m = memory_attention(q_m, mem, g_mem[l], w_mk[l], w_mv[l], g_qm[l], g_km[l])
        y = jnp.concatenate([
            y_a.reshape(B, S, A_WIDTH) * jax.nn.silu(z_a),
            y_b.reshape(B, S, B_WIDTH) * jax.nn.silu(z_b),
            y_m.reshape(B, S, M_WIDTH) * jax.nn.silu(z_m),
        ], axis=-1)
        x = x + y @ w_out[l]
    return x


_drawn_inputs = setup_inputs


def setup_inputs(seed=0):
    import zlib

    import numpy as np

    out = dict(_drawn_inputs(seed))
    spreads = {}
    factors = {'g_cq': 8.0,
     'g_ckv': 7.156,
     'g_qa': 6.445,
     'g_ka': 5.525,
     'g_qb': 8.0,
     'g_kb': 8.0,
     'g_mem': 8.0,
     'g_qm': 8.0,
     'g_km': 8.0}
    for name, (base, spread) in spreads.items():
        noise = np.random.default_rng([zlib.crc32(name.encode()), seed]).standard_normal(out[name].shape)
        drawn = base * np.exp(spread * noise) if base else spread * noise
        out[name] = __import__('jax').numpy.asarray(drawn.astype(out[name].dtype))
    for name, factor in factors.items():
        out[name] = (out[name] * factor).astype(out[name].dtype)
    return out
```

```python
import concourse.bass as bass
from concourse import mybir
from contextlib import ExitStack

F32 = mybir.dt.float32
F32R = mybir.dt.float32r
ALU = mybir.AluOpType
ACT = mybir.ActivationFunctionType
AX = mybir.AxisListType

P = 128
SEQ, DM, NMEM = 512, 1024, 256
NT, KC = SEQ // P, DM // P
EPS = 1e-6
HD = 64
AH, BH, MH, IH = 6, 6, 4, 8
BD, ROPE = 96, 32
QL, KVL = 256, 128
TOPK = 128
W_WIDTH = 512
N_RAW, N_SPLIT = 6, 6
N_RELU = 3
LEAD_HI, LEAD = 4, 3
MARK, INADMISSIBLE, MARKED_BELOW = -3.4e38, -3.0e38, -3.2e38
NEG = -1.0e30
A_SCALE, B_SCALE, M_SCALE = HD ** -0.5, BD ** -0.5, HD ** -0.5

G_IN, G_MEM, G_CQ, G_CKV, G_QA, G_KA, G_QM, G_KM, GAIN_COLS = 0, 8, 16, 18, 19, 20, 21, 22, 23

GROUPS = [
    ("idx", 1152, 512, True), ("kwz", 1664, 488, False), ("c", 2120, 384, True),
    ("mem", 0, 512, False), ("zb", 2536, 384, False), ("ka", 384, 384, False), ("qa", 0, 384, True),
    ("va", 768, 384, False), ("qm", 2920, 256, True), ("zm", 3176, 256, False),
    ("out0", 0, 512, False), ("out1", 512, 512, False),
]
K_ROPE = 2504
NAMES = [g[0] for g in GROUPS]
N_IN_CHUNKS = KC * NAMES.index("out0")
N_CHUNKS = KC * len(GROUPS)
OUT_ORDER = [3, 4, 5, 0, 1, 2, 6, 7]


def last_chunk(name):
    return KC * NAMES.index(name) + KC - 1


def attention_units():
    units = []
    for i, heads in enumerate([[(0, 1, 2), (3, 4, 5)], [(0, 1), (2, 3), (4, 5)]] + 2 * [[(h,) for h in range(6)]]):
        units += [("B", i, hs, P * (i + 1)) for hs in heads]
    for i, heads in enumerate([[(0, 2, 4), (1, 3, 5)], [(0, 2), (1, 3), (4,), (5,)]] + 2 * [[(h,) for h in range(6)]]):
        units += [("A", i, hs, P * (i + 1)) for hs in heads]
    units += [("M", i, hs, NMEM) for i in range(NT) for hs in [(0, 2), (1, 3)]]
    return units


N_UNITS = len(attention_units())
TOPK_FIRST, TOPK_TWO = 24, (28, 29, 30, 32, 33, 36, 37, 41)
FIRST_STEP = 43
TWO_STEPS_FROM = 80
TRANSPOSE, WEIGH, SCALE_GATE, SCALE_Y, TURN_Y = 2, 3, 1, 3, 5
N_STEPS = N_UNITS + TURN_Y


def schedule():
    at = {c: [] for c in range(N_CHUNKS)}
    at[8].append(("x_norm",))
    at[11].append(("mem_norm",))
    for name in NAMES:
        at[last_chunk(name)].append(("evac", name))
    at[last_chunk("kwz") + 1].append(("krope",))
    at[last_chunk("kwz") + 2].append(("kidx_T",))
    for u in range(3 * IH):
        at[last_chunk("kwz") + 4 + u // 4].append(("rel", u))
    at[last_chunk("c") + 3].append(("c_sum",))
    for t in range(NT):
        at[last_chunk("c") + 4 + 4 * t].append(("b_proj", t))
        at[last_chunk("c") + 6 + 4 * t].append(("b_scale", t))
        at[last_chunk("c") + 8 + 4 * t].append(("b_T", t))
    at[last_chunk("mem") + 2].append(("km_norm",))
    at[last_chunk("mem") + 5].append(("km_scale",))
    at[last_chunk("mem") + 21].append(("km_T",))
    at[last_chunk("ka") + 1].append(("ka_sums",))
    at[last_chunk("ka") + 2].append(("ka_norm",))
    at[last_chunk("ka") + 4].append(("ka_scale",))
    at[last_chunk("ka") + 6].append(("ka_T",))
    at[last_chunk("qa") + 3].append(("qa_sum",))
    at[last_chunk("qm") + 3].append(("qm_sum",))
    for s in range(N_STEPS):
        c = FIRST_STEP + s
        if c >= TWO_STEPS_FROM:
            c = TWO_STEPS_FROM + (c - TWO_STEPS_FROM) // 2
        at[c].append(("step", s))
    at[last_chunk("c") + 1].append(("distances", 0))
    left = {i: TOPK // 8 for i in range(1, NT)}
    for c in range(TOPK_FIRST, N_IN_CHUNKS):
        kinds = [e[0] for e in at[c]]
        n = 0 if "b_proj" in kinds or "ka_norm" in kinds else 1 + (c in TOPK_TWO)
        for _ in range(n):
            tiles = [i for i in left if left[i] and c >= TOPK_FIRST + 2 * (i - 1)]
            if not tiles:
                break
            i = tiles[(c + _) % min(2, len(tiles))]
            at[c].append(("topk", i))
            left[i] -= 1
            if not left[i]:
                at[c].append(("distances", i))
    assert not any(left.values())
    return at


def score_at(i):
    return P * i * (i + 1) // 2


def build_layer(nc, x, xT, mem, memT, w_in, w_uq, w_ukv, w_mk, w_mv, w_out, gains, tables, out):
    at = schedule()
    units = attention_units()
    ctx = ExitStack()
    with ctx:
        base = [nc.sbuf_base + 31 & ~31]
        arena_bytes = nc.sbuf_usable_end - base[0] - 64
        ctx.enter_context(nc.sbuf_tensor("arena", [P, arena_bytes], mybir.dt.uint8))

        def place(name, shape, dt=F32, over=None, skip=0):
            size = 4
            for n in shape:
                size *= n
            if over is None:
                offset = base[0]
                base[0] += (size + 31) // 32 * 32
            else:
                offset = over + skip
            assert base[0] <= nc.sbuf_usable_end, (name, base[0])
            return nc.alloc_sbuf_tensor_at(name, [P] + list(shape), dt, offset=offset), offset

        x_nat, at_x = place("x_nat", [NT, DM])
        hT_hi, at_hT = place("hT_hi", [KC, SEQ], F32R)
        hT_lo, at_hT_lo = place("hT_lo", [KC, SEQ], F32R)
        x_res, _ = place("x_res", [NT, DM], F32, at_hT)
        w_raw, _ = place("w_raw", [N_RAW, W_WIDTH])
        w_hi, _ = place("w_hi", [N_SPLIT, W_WIDTH], F32R)
        w_lo, _ = place("w_lo", [N_SPLIT, W_WIDTH], F32R)
        gates, at_gates = place("gates", [NT, DM])
        xT_raw, _ = place("xT_raw", [KC, SEQ], F32, at_gates)
        qbT, at_qb = place("qbT", [BH, SEQ])
        qidx_parts, _ = place("qidx_parts", [IH, SEQ], F32R, at_qb)
        kidx_hi, _ = place("kidx_hi", [SEQ], F32R, at_qb, 4 * IH * SEQ)
        kidx_lo, _ = place("kidx_lo", [SEQ], F32R, at_qb, 4 * (IH + 1) * SEQ)
        yT = {}
        for branch, n, over in [("B", 3, at_x), ("A", 3, at_qb), ("M", 2, at_hT_lo)]:
            yT[branch] = [place(f"y{branch}T_{part}", [n, SEQ], F32R, over, 4 * n * SEQ * m)[0]
                          for m, part in enumerate(["hi", "lo"])]
        kbT, at_kb = place("kbT", [BH, SEQ])
        memT_raw, _ = place("memT_raw", [KC, NMEM], F32, at_qb, 4 * (IH + 2) * SEQ)
        vb, _ = place("vb", [NT, BH * HD])
        va, at_va = place("va", [NT, AH * HD])
        qaT, _ = place("qaT", [3, SEQ])
        kaT, _ = place("kaT", [3, SEQ])
        ka_nat, _ = place("ka_nat", [NT, AH * HD], F32, at_va)
        mT_hi, _ = place("mT_hi", [KC, NMEM], F32R, at_va)
        mT_lo, _ = place("mT_lo", [KC, NMEM], F32R, at_va, 4 * KC * NMEM)
        qmT, _ = place("qmT", [2, SEQ])
        kmT, _ = place("kmT", [2, NMEM])
        kvm, _ = place("kvm", [2, 512])
        w_idx, _ = place("w_idx", [NT, IH])
        uq, _ = place("uq", [2, BH * BD])
        ukv, _ = place("ukv", [BH * 2 * HD])
        score, _ = place("score", [score_at(NT)])
        prob, at_prob = place("prob", [3, 512])
        probT, at_probT = place("probT", [3, 512])
        cT, _ = place("cT", [3, SEQ], F32, at_probT)
        mem_nat, _ = place("mem_nat", [2, DM], F32, at_prob)
        squares, _ = place("squares", [DM], F32, at_probT, 2048)
        bias_ring, at_bias = place("bias_ring", [1152])
        relu_ring, _ = place("relu_ring", [N_RELU, 512], F32, at_prob)
        kidx_nat, _ = place("kidx_nat", [NT, 2 * HD], F32, at_bias)
        q_nat, _ = place("q_nat", [BH, BD], F32, at_bias)
        k_nat, _ = place("k_nat", [BH, BD], F32, at_bias, 4 * BH * BD)
        qsT, at_c = place("qsT", [3, SEQ])
        kvm_sq, _ = place("kvm_sq", [2, MH * HD], F32, at_c)
        ka_sq, _ = place("ka_sq", [NT, AH * HD], F32, at_c)
        head_sq, at_hsq = place("head_sq", [960])
        rope_tmp, _ = place("rope_tmp", [2, BH, ROPE], F32, at_hsq)
        krope, _ = place("krope", [NT, ROPE])
        krot, _ = place("krot", [NT, ROPE])
        krot_tmp, _ = place("krot_tmp", [2, NT, ROPE], F32, at_hsq)
        gain, _ = place("gain", [GAIN_COLS + 2 * BD])
        tab, _ = place("tab", [P + 64 * NT + 3 + 512 + AH * NT])
        half, _ = place("half", [32])
        minus_one, _ = place("minus_one", [BH])
        table_load, _ = place("table_load", [1])
        kgain, _ = place("kgain", [2])
        qb_row, _ = place("qb_row", [BD])
        ssx, _ = place("ssx", [NT + 2])
        msx, _ = place("msx", [NT + 2])
        rx, _ = place("rx", [NT + 2])
        rx2, _ = place("rx2", [NT])
        irx, _ = place("irx", [NT])
        css, _ = place("css", [NT, 2])
        cr, _ = place("cr", [NT, 2])
        cr2, _ = place("cr2", [NT, 2])
        krss, _ = place("krss", [NT])
        bss, _ = place("bss", [NT, 2 * BH])
        br, _ = place("br", [NT, 3 * BH])
        kss, _ = place("kss", [NT * AH + 2 * MH])
        kr, _ = place("kr", [NT * AH + 2 * MH])
        qms, _ = place("qms", [NT * AH + NT * MH])
        qr, _ = place("qr", [NT * AH + NT * MH])
        slope_r, _ = place("slope_r", [NT * AH])
        top8, _ = place("top8", [3, 8])
        rowmax, _ = place("rowmax", [NT * 16])
        negmax, _ = place("negmax", [NT * 16])
        rowsum, _ = place("rowsum", [NT * 16])
        rowinv, _ = place("rowinv", [NT * 16])

        ident = tab[:, 0:P]
        rope_tab = tab[:, P:P + 64 * NT].rearrange("p (t c) -> p t c", t=NT)
        ones2 = tab[:, P + 64 * NT:P + 64 * NT + 2]
        ones1 = tab[:, P + 64 * NT + 2:P + 64 * NT + 3]
        ndist = tab[:, P + 64 * NT + 3:P + 64 * NT + 3 + 512]
        slopes = tab[:, P + 64 * NT + 515:P + 64 * NT + 515 + AH * NT]

        psum = [ctx.enter_context(nc.psum_tensor(f"bank{b}", [P, 512], F32)) for b in range(8)]

        uses, fills, frees = {}, [0] * 8, [0] * 8

        def take(bank, key, filled=1, freed=1):
            uses[key] = (bank, fills[bank], frees[bank])
            fills[bank] += filled
            frees[bank] += freed

        def banks_of(name):
            _, _, cols, transposed = GROUPS[NAMES.index(name)]
            return 2 if name == "mem" else cols // P if transposed else NT

        def take_banks(event):
            kind = event[0]
            if kind == "kidx_T":
                take(4, event)
            if kind == "rel":
                take(4 + event[1] % 4, event)
            if kind == "ka_T":
                for j in range(3):
                    take(4 + j, (kind, j))
            if kind == "b_proj":
                for j in range(4):
                    take(4 + j, ("b_proj", event[1], j))
            if kind == "b_T":
                for j in range(3):
                    take(4 + j, ("b_T", event[1], j))
            if kind in ("c_sum", "km_T", "qa_sum", "qm_sum"):
                take(6, event)
            if kind == "step":
                s = event[1]
                if s - TURN_Y in last_unit:
                    take(6, ("y_T",) + last_unit[s - TURN_Y])
                if 0 <= s - TRANSPOSE < N_UNITS:
                    take(6, ("PT", s - TRANSPOSE))
                if s < N_UNITS:
                    take(4 + s % 2, ("S", s))
                if s - WEIGH in first_unit:
                    take(7, ("O",) + first_unit[s - WEIGH], filled=0)

        first_unit, last_unit = {}, {}
        for u, (branch, i, _, _) in enumerate(units):
            if u == 0 or units[u - 1][:2] != (branch, i):
                first_unit[u] = (branch, i)
            if u == N_UNITS - 1 or units[u + 1][:2] != (branch, i):
                last_unit[u] = (branch, i)
        y_number = {group: n for n, group in enumerate(last_unit.values())}
        for c in range(N_CHUNKS):
            if c % KC == 0:
                for j in range(banks_of(NAMES[c // KC])):
                    take(j + 4 * (NAMES[c // KC] == "kwz"), ("acc", NAMES[c // KC], j))
            for event in at[c]:
                take_banks(event)

        def sem(name):
            return ctx.enter_context(nc.semaphore(name))

        bank_filled = [sem(f"bank_filled{b}") for b in range(8)]
        bank_free = [sem(f"bank_free{b}") for b in range(8)]
        xT_in = [sem(f"xT_in{k}") for k in range(KC)]
        raw_in = [sem(f"raw_in{s}") for s in range(N_RAW)]
        x_in, mem_in, memT_in, uw_in = sem("x_in"), sem("mem_in"), sem("memT_in"), sem("uw_in")
        gain_in, tab_in, stored = sem("gain_in"), sem("tab_in"), sem("stored")
        hi_ready, lo_ready, chunk_used = sem("hi_ready"), sem("lo_ready"), sem("chunk_used")
        act_own, dve_own, pool_own = sem("act_own"), sem("dve_own"), sem("pool_own")
        sums_ready, root_ready = sem("sums_ready"), sem("root_ready")
        xT_hi_ready, xT_lo_ready = sem("xT_hi_ready"), sem("xT_lo_ready")
        mT_hi_ready, mT_lo_ready = sem("mT_hi_ready"), sem("mT_lo_ready")
        relu_used, krot_ready, km_ready, ka_ready = sem("relu_used"), sem("krot_ready"), sem("km_ready"), sem("ka_ready")
        squares_ready, b_scalar_done, b_nat_ready = sem("squares_ready"), sem("b_scalar_done"), sem("b_nat_ready")
        consts_ready, dist_ready, bias_ready = sem("consts_ready"), sem("dist_ready"), sem("bias_ready")
        max_ready, exp_ready, pv_done = sem("max_ready"), sem("exp_ready"), sem("pv_done")
        pool_squares, gate_scaled = sem("pool_squares"), sem("gate_scaled")
        kidx_ready, idx_hi_ready = sem("kidx_ready"), sem("idx_hi_ready")
        yT_hi_ready = sem("yT_hi_ready")

        def wait_filled(eng, key):
            bank, n, _ = uses[key]
            eng.wait_ge(bank_filled[bank], n + 1)
            return psum[bank]

        def wait_copied(eng, key):
            bank, _, n = uses[key]
            eng.wait_ge(bank_free[bank], n + 1)

        def wait_free(eng, key):
            bank, _, n = uses[key]
            if n:
                eng.wait_ge(bank_free[bank], n)
            return psum[bank]

        def filled(key):
            return bank_filled[uses[key][0]]

        def free(key):
            return bank_free[uses[key][0]]

        def wait_chunk_used(eng, c):
            g, k = divmod(c, KC)
            if k == KC - 1:
                wait_filled(eng, ("acc", NAMES[g], banks_of(NAMES[g]) - 1))
            else:
                eng.wait_ge(chunk_used, (KC - 1) * g + k + 1)

        by_bank = ("c_sum", "qa_sum", "qm_sum")
        roots = [e for c in range(N_CHUNKS) for e in at[c] if e[0] in
                 ("x_norm", "mem_norm", "km_norm", "ka_norm", "b_proj") + by_bank]
        sums = [e for e in roots if e[0] not in by_bank]
        squared = [("km",)] + [("ka", t) for t in range(NT)] + [("qa", j) for j in range(3)] + [("qm", j) for j in range(2)]
        a_units = [u for u in range(N_UNITS) if units[u][0] == "A"]

        def wait_root(eng, key):
            eng.wait_ge(root_ready, roots.index(key) + 1)

        def gain_of(c):
            g, k = divmod(c, KC)
            if NAMES[g].startswith("out"):
                return None
            col = (G_MEM if NAMES[g] == "mem" else G_IN) + k
            return gain[:, col:col + 1]

        def tile(t):
            return slice(P * t, P * t + P)

        def stat(branch, i, h):
            return i * BH + h if branch == "B" else NT * BH + i * MH + h if branch == "M" \
                else NT * (BH + MH) + i * AH + h

        def stats_of(branch, i, heads):
            step = heads[1] - heads[0] if len(heads) > 1 else 1
            return slice(stat(branch, i, heads[0]), stat(branch, i, heads[-1]) + 1, step)

        def score_scale(branch, i, heads):
            step = heads[1] - heads[0] if len(heads) > 1 else 1
            if branch == "B":
                return br[:, i, heads[0]:heads[-1] + 1:step]
            col = i * AH if branch == "A" else NT * AH + i * MH
            return qr[:, col + heads[0]:col + heads[-1] + 1:step]

        y_cols = {"A": (0, 3), "B": (3, 3), "M": (6, 2)}

        block = ctx.enter_context(nc.Block())

        @block.sync
        def _(sp):
            for c in range(N_CHUNKS):
                g, k = divmod(c, KC)
                name, first, cols, _ = GROUPS[g]
                s = c % N_RAW
                if c < KC:
                    sp.dma_start(xT_raw[:, c, :], xT[P * c:P * c + P, :]).then_inc(xT_in[c], 16)
                if c >= N_RAW:
                    sp.wait_ge(lo_ready, c - N_RAW + 1)
                if name == "mem":
                    sp.dma_start(w_raw[:, s, 0:256], w_mk[P * k:P * k + P, :]).then_inc(raw_in[s], 16)
                    sp.dma_start(w_raw[:, s, 256:512], w_mv[P * k:P * k + P, :]).then_inc(raw_in[s], 16)
                elif name == "kwz":
                    sp.dma_start(w_raw[:, s, 0:cols - ROPE], w_in[P * k:P * k + P, first:first + cols - ROPE])\
                        .then_inc(raw_in[s], 16)
                    sp.dma_start(w_raw[:, s, cols - ROPE:cols], w_in[P * k:P * k + P, K_ROPE:K_ROPE + ROPE])\
                        .then_inc(raw_in[s], 16)
                elif name.startswith("out"):
                    row = P * OUT_ORDER[k]
                    sp.dma_start(w_raw[:, s, 0:cols], w_out[row:row + P, first:first + cols]).then_inc(raw_in[s], 16)
                else:
                    sp.dma_start(w_raw[:, s, 0:cols], w_in[P * k:P * k + P, first:first + cols])\
                        .then_inc(raw_in[s], 16)
                if c == KC - 1:
                    sp.dma_start(x_nat[:, :, :], x.rearrange("(t p) d -> p t d", p=P)).then_inc(x_in, 16)
                if c == N_IN_CHUNKS + N_RAW:
                    wait_filled(sp, ("acc", NAMES[N_IN_CHUNKS // KC - 1], NT - 1))
                    sp.dma_start(x_res[:, :, :], x.rearrange("(t p) d -> p t d", p=P)).then_inc(x_in, 16)
                if c == KC + 1:
                    sp.dma_start(mem_nat[:, :, :], mem.rearrange("(t p) d -> p t d", p=P)).then_inc(mem_in, 16)
                if c == KC + 3:
                    sp.dma_start(memT_raw[:, :, :], memT.rearrange("(k p) n -> p k n", p=P)).then_inc(memT_in, 16)
                if c == KC + 6:
                    sp.dma_start(uq[:, :, :], w_uq.rearrange("(k p) n -> p k n", p=P)).then_inc(uw_in, 16)
                    sp.dma_start(ukv[:, :], w_ukv).then_inc(uw_in, 16)
            ov = out.rearrange("(t p) d -> p t d", p=P)
            for n in range(2 * NT):
                side, t = divmod(n, NT)
                wait_copied(sp, ("acc", f"out{side}", t))
                sp.dma_start(ov[:, t, 512 * side:512 * side + 512],
                             x_res[:, t, 512 * side:512 * side + 512]).then_inc(stored, 16)
            sp.wait_ge(stored, 16 * 2 * NT)

        def raw_loads(c):
            return 16 * sum(2 if NAMES[e // KC] in ("mem", "kwz") else 1 for e in range(c % N_RAW, c + 1, N_RAW))

        @block.gpsimd
        def _(pool):
            own = [0]

            def then(ins):
                own[0] += 1
                ins.then_inc(pool_own, 1)
                pool.wait_ge(pool_own, own[0])

            nc.gpsimd.memset(minus_one[:, :], -1.0)
            then(nc.gpsimd.memset(half[:, :], -0.5))

            def mean(dst, src, n):
                then(nc.gpsimd.tensor_scalar(dst, src, 1.0 / n, EPS, ALU.mult, ALU.add))

            def power(dst, src):
                return nc.gpsimd.tensor_tensor(dst, src, half[:, 0:src.shape[-1]], ALU.pow)

            def times(dst, src, factor):
                return nc.gpsimd.tensor_scalar(dst, src, factor, None, ALU.mult)

            def root_of(key):
                if roots.index(key):
                    pool.wait_ge(root_ready, roots.index(key))
                if key in sums:
                    pool.wait_ge(sums_ready, sums.index(key) + 1)
                else:
                    wait_copied(pool, key)
                if key[0] == "x_norm":
                    x = slice(0, NT)
                    mean(msx[:, x], ssx[:, x], DM)
                    then(power(rx[:, x], msx[:, x]))
                    nc.gpsimd.tensor_tensor(rx2[:, :], rx[:, x], rx[:, x], ALU.mult)
                    nc.gpsimd.tensor_tensor(irx[:, :], msx[:, x], rx[:, x], ALU.mult).then_inc(root_ready, 1)
                if key[0] == "mem_norm":
                    m = slice(NT, NT + 2)
                    mean(msx[:, m], ssx[:, m], DM)
                    power(rx[:, m], msx[:, m]).then_inc(root_ready, 1)
                if key[0] == "c_sum":
                    mean(cr[:, :, 0], css[:, :, 0], QL)
                    mean(cr[:, :, 1], css[:, :, 1], KVL)
                    both = cr[:, :, :].rearrange("p t a -> p (t a)")
                    then(power(both, both))
                    then(nc.gpsimd.tensor_tensor(cr[:, :, :], cr[:, :, :],
                                                 rx[:, 0:NT].unsqueeze(2).broadcast_to([P, NT, 2]), ALU.mult))
                    nc.gpsimd.tensor_tensor(cr2[:, :, :], cr[:, :, :], cr[:, :, :], ALU.mult).then_inc(root_ready, 1)
                if key[0] == "b_proj":
                    t = key[1]
                    q, k = bss[:, t, 0:BH], bss[:, t, BH:2 * BH]
                    pool.wait_ge(krot_ready, 1)
                    nc.gpsimd.tensor_scalar(q, q, cr2[:, t, 0:1], None, ALU.mult)
                    then(nc.gpsimd.tensor_scalar(k, k, cr2[:, t, 1:2], krss[:, t:t + 1], ALU.mult, ALU.add))
                    mean(br[:, t, 0:2 * BH], bss[:, t, :], BD)
                    then(power(br[:, t, 0:2 * BH], br[:, t, 0:2 * BH]))
                    nc.gpsimd.tensor_scalar(br[:, t, 0:BH], br[:, t, 0:BH], cr[:, t, 0:1], B_SCALE, ALU.mult, ALU.mult)
                    nc.gpsimd.tensor_scalar(br[:, t, 2 * BH:], br[:, t, BH:2 * BH], cr[:, t, 1:2], None, ALU.mult)\
                        .then_inc(root_ready, 1)
                if key[0] == "km_norm":
                    mean(kr[:, NT * AH:], kss[:, NT * AH:], HD)
                    power(kr[:, NT * AH:], kr[:, NT * AH:]).then_inc(root_ready, 1)
                if key[0] == "ka_norm":
                    mean(kr[:, 0:NT * AH], kss[:, 0:NT * AH], HD)
                    power(kr[:, 0:NT * AH], kr[:, 0:NT * AH]).then_inc(root_ready, 1)
                if key[0] in ("qa_sum", "qm_sum"):
                    n, heads, scale = (slice(0, NT * AH), AH, A_SCALE) if key[0] == "qa_sum" else \
                        (slice(NT * AH, NT * AH + NT * MH), MH, M_SCALE)
                    ms, root = qms[:, n], qr[:, n]
                    mean(ms, ms, HD)
                    then(power(root, ms))
                    if key[0] == "qa_sum":
                        then(nc.gpsimd.tensor_tensor(slope_r[:, :], ms, root, ALU.mult))
                        by_tile = slope_r[:, :].rearrange("p (t h) -> p t h", t=NT)
                        then(nc.gpsimd.tensor_tensor(by_tile, by_tile,
                                                     irx[:, :].unsqueeze(2).broadcast_to([P, NT, AH]), ALU.mult))
                        then(nc.gpsimd.tensor_tensor(slope_r[:, :], slope_r[:, :], slopes, ALU.mult))
                    by_tile = root.rearrange("p (t h) -> p t h", t=NT)
                    then(nc.gpsimd.tensor_tensor(by_tile, by_tile,
                                                 rx[:, 0:NT].unsqueeze(2).broadcast_to([P, NT, heads]), ALU.mult))
                    nc.gpsimd.tensor_scalar(root, root, scale, None, ALU.mult).then_inc(root_ready, 1)

            def bias_of(u):
                _, i, heads, keys = units[u]
                n = a_units.index(u)
                if n >= 2:
                    pool.wait_ge(max_ready, u - 1)
                if u in first_unit:
                    pool.wait_ge(dist_ready, i + 1)
                for m, h in enumerate(heads):
                    at_head = n % 2 * 512 + keys * m
                    ins = nc.gpsimd.tensor_tensor(
                        bias_ring[:, at_head:at_head + keys], score[:, score_at(i):score_at(i) + keys],
                        slope_r[:, i * AH + h:i * AH + h + 1].broadcast_to([P, keys]), ALU.mult)
                ins.then_inc(bias_ready, 1)

            def squares_of(event):
                if event == ("evac", "mem"):
                    wait_copied(pool, ("acc", "mem", 1))
                    square(kvm_sq[:, :, :], kvm[:, :, 0:MH * HD])
                if event == ("evac", "ka"):
                    for t in range(NT):
                        wait_copied(pool, ("acc", "ka", t))
                        square(ka_sq[:, t, :], ka_nat[:, t, :])
                if event in (("evac", "qa"), ("evac", "qm")):
                    name = event[1]
                    for j in range(banks_of(name)):
                        wait_copied(pool, ("acc", name, j))
                        q = (qaT if name == "qa" else qmT)[:, j, :]
                        square(qsT[:, j, :], q)

            def square(dst, src):
                nc.gpsimd.tensor_tensor(dst, src, src, ALU.mult).then_inc(pool_squares, 1)

            def scale_gate(u):
                branch, i = last_unit[u]
                first, n = y_cols[branch]
                heads = 2 * n
                cols = slice(stat(branch, i, 0), stat(branch, i, 0) + heads)
                if branch == "A":
                    pool.wait_ge(exp_ready, a_units.index(u) + 1)
                else:
                    wait_copied(pool, ("S", u))
                wait_copied(pool, ("acc", {"A": "kwz", "B": "zb", "M": "zm"}[branch], i))
                then(nc.gpsimd.tensor_tensor(rowinv[:, cols], rowsum[:, cols], minus_one[:, 0:heads], ALU.pow))
                y = gates[:, i, P * first:P * (first + n)].rearrange("p (h d) -> p h d", h=heads)
                nc.gpsimd.tensor_tensor(y, y, rowinv[:, cols].unsqueeze(2).broadcast_to([P, heads, HD]), ALU.mult)\
                    .then_inc(gate_scaled, 1)

            for c in range(N_CHUNKS):
                for event in at[c]:
                    squares_of(event)
                    if event[0] == "step" and event[1] - SCALE_GATE in last_unit:
                        scale_gate(event[1] - SCALE_GATE)
                    if event in roots:
                        root_of(event)
                    if event[0] == "step" and event[1] + 2 in a_units:
                        bias_of(event[1] + 2)

        @block.scalar
        def _(act):
            act.dma_start(gain[:, :], gains).then_inc(gain_in, 16)
            act.dma_start(tab[:, :], tables).then_inc(tab_in, 16)
            own = [0]

            def mark(ins):
                own[0] += 1
                ins.then_inc(act_own, 1)
                return own[0]

            def split_hi(c):
                cols = GROUPS[c // KC][2]
                act.wait_ge(raw_in[c % N_RAW], raw_loads(c))
                if c >= N_SPLIT:
                    wait_chunk_used(act, c - N_SPLIT)
                factor = 1.0 if gain_of(c) is None else gain_of(c)
                nc.scalar.activation(w_hi[:, c % N_SPLIT, 0:cols], w_raw[:, c % N_RAW, 0:cols],
                                     ACT.Copy, scale=factor).then_inc(hi_ready, 1)

            def x_hi(k):
                act.wait_ge(xT_in[k], 16)
                nc.scalar.activation(hT_hi[:, k, :], xT_raw[:, k, :], ACT.Copy).then_inc(xT_hi_ready, 1)

            def copy_out(key, dst, src, func=ACT.Copy, **kw):
                nc.scalar.activation(dst, src, func, **kw).then_inc(free(key), 1)

            act.wait_ge(pool_own, 1)
            nc.scalar.activation(table_load[:, :], half[:, 0:1], ACT.Copy)

            def scalar_event(event):
                kind = event[0]
                if kind == "x_norm":
                    act.wait_ge(x_in, 16)
                    for t in range(NT):
                        ins = nc.scalar.activation(squares[:, :], x_nat[:, t, :], ACT.Square, accum_out=ssx[:, t:t + 1])
                        if t < NT - 1:
                            act.wait_ge(act_own, mark(ins))
                    ins.then_inc(sums_ready, 1)
                if kind == "mem_norm":
                    act.wait_ge(mem_in, 16)
                    act.wait_ge(sums_ready, 1)
                    act.wait_ge(act_own, mark(nc.scalar.activation(
                        squares[:, :], mem_nat[:, 0, :], ACT.Square, accum_out=ssx[:, NT:NT + 1])))
                    nc.scalar.activation(squares[:, :], mem_nat[:, 1, :], ACT.Square,
                                         accum_out=ssx[:, NT + 1:NT + 2]).then_inc(sums_ready, 1)
                    act.wait_ge(memT_in, 16)
                    for n in range(4):
                        nc.scalar.activation(mT_hi[:, 2 * n:2 * n + 2, :], memT_raw[:, 2 * n:2 * n + 2, :], ACT.Copy)\
                            .then_inc(mT_hi_ready, 1)
                if kind == "evac" and not event[1].startswith("out"):
                    name = event[1]
                    if name == "kwz":
                        wait_root(act, ("x_norm",))
                    if name == "mem":
                        wait_root(act, ("mem_norm",))
                    if name == "c":
                        act.wait_ge(sums_ready, 2)
                    if name == "kwz":
                        for j in range(NT):
                            bank = wait_filled(act, ("acc", name, j))
                            nc.scalar.activation(kidx_nat[:, j, :].rearrange("p (a d) -> p a d", a=2),
                                                 bank[:, 0:HD].unsqueeze(1).broadcast_to([P, 2, HD]), ACT.Copy,
                                                 scale=rx[:, j:j + 1]).then_inc(kidx_ready, 1)
                    for j in range(banks_of(name)):
                        key = ("acc", name, j)
                        bank = wait_filled(act, key)
                        r = rx[:, j:j + 1]
                        if name == "idx":
                            for part in (slice(0, HD), slice(HD, P)):
                                h = 2 * j + part.start // HD
                                nc.scalar.activation(qidx_parts[part, h, :], bank[part, :], ACT.Copy)\
                                    .then_inc(idx_hi_ready, 1)
                        if name == "kwz":
                            nc.scalar.activation(w_idx[:, j, :], bank[:, HD:HD + IH], ACT.Copy, scale=rx2[:, j:j + 1])
                            nc.scalar.activation(krope[:, j, :], bank[:, 456:488], ACT.Copy, scale=r)
                            copy_out(key, gates[:, j, 0:384], bank[:, HD + IH:456], ACT.Silu, scale=r)
                        if name == "c":
                            nc.scalar.activation(qsT[:, j, :], bank[:, :], ACT.Square)
                            copy_out(key, cT[:, j, :], bank[:, :], scale=gain[:, G_CQ + j:G_CQ + j + 1])
                        if name == "mem":
                            copy_out(key, kvm[:, j, :], bank[:, :], scale=rx[:, NT + j:NT + j + 1])
                        if name == "zb":
                            copy_out(key, gates[:, j, 384:768], bank[:, 0:384], ACT.Silu, scale=r)
                        if name == "ka":
                            copy_out(key, ka_nat[:, j, :], bank[:, 0:384], scale=r)
                        if name == "qa":
                            copy_out(key, qaT[:, j, :], bank[:, :])
                        if name == "va":
                            copy_out(key, va[:, j, :], bank[:, 0:384], scale=r)
                        if name == "qm":
                            copy_out(key, qmT[:, j, :], bank[:, :])
                        if name == "zm":
                            copy_out(key, gates[:, j, 768:1024], bank[:, 0:256], ACT.Silu, scale=r)
                if kind == "kidx_T":
                    nc.scalar.activation(kidx_hi[:, :], wait_filled(act, event)[:, :], ACT.Copy)\
                        .then_inc(idx_hi_ready, 1)
                if kind == "rel":
                    u = event[1]
                    keys = P * (2 + u // IH)
                    bank = wait_filled(act, event)
                    if u >= N_RELU:
                        act.wait_ge(relu_used, u - N_RELU + 1)
                    copy_out(event, relu_ring[:, u % N_RELU, 0:keys], bank[:, 0:keys], ACT.Relu)
                if kind == "b_proj":
                    t = event[1]
                    if t:
                        act.wait_ge(b_nat_ready, t)
                    for j in range(2):
                        bank = wait_filled(act, (kind, t, j))
                        nc.scalar.activation(head_sq[:, 288 * j:288 * j + 288], bank[:, 0:288], ACT.Square)
                    for j in range(2):
                        bank = wait_filled(act, (kind, t, 2 + j))[:, 0:384].rearrange("p (h c) -> p h c", h=3)
                        ins = nc.scalar.activation(
                            head_sq[:, 576 + 192 * j:768 + 192 * j].rearrange("p (h d) -> p h d", h=3),
                            bank[:, :, 0:HD], ACT.Square)
                    ins.then_inc(squares_ready, 1)
                    wait_root(act, ("c_sum",))
                    for j in range(2):
                        bank = psum[6 + j][:, 0:384].rearrange("p (h c) -> p h c", h=3)
                        ins = nc.scalar.activation(vb[:, t, 192 * j:192 * j + 192].rearrange("p (h d) -> p h d", h=3),
                                                   bank[:, :, HD:2 * HD], ACT.Copy, scale=cr[:, t, 1:2])
                    ins.then_inc(b_scalar_done, 1)
                if kind == "b_T":
                    t = event[1]
                    for j in range(3):
                        key = (kind, t, j)
                        bank = wait_filled(act, key)[0:BD, :].rearrange("p (h n) -> p h n", h=4)
                        if j == 0:
                            copy_out(key, qbT[0:BD, 0:4, tile(t)], bank)
                        if j == 1:
                            nc.scalar.activation(qbT[0:BD, 4:6, tile(t)], bank[:, 0:2, :], ACT.Copy)
                            copy_out(key, kbT[0:BD, 0:2, tile(t)], bank[:, 2:4, :])
                        if j == 2:
                            copy_out(key, kbT[0:BD, 2:6, tile(t)], bank)
                if kind == "km_T":
                    copy_out(event, kmT[:, :, :].rearrange("p j n -> p (j n)"), wait_filled(act, event)[:, :],
                             scale=kgain[:, 1:2])
                if kind == "ka_T":
                    for j in range(3):
                        copy_out((kind, j), kaT[:, j, :], wait_filled(act, (kind, j))[:, :], scale=kgain[:, 0:1])

                if kind == "step":
                    s = event[1]
                    if s - TURN_Y in last_unit:
                        branch, i = last_unit[s - TURN_Y]
                        first, n = y_cols[branch]
                        bank = wait_filled(act, ("y_T", branch, i))
                        nc.scalar.activation(yT[branch][0][:, :, tile(i)],
                                             bank[:, 0:P * n].rearrange("p (k n) -> p k n", k=n), ACT.Copy)\
                            .then_inc(yT_hi_ready, 1)
                    if 0 <= s - TRANSPOSE < N_UNITS:
                        u = s - TRANSPOSE
                        n = units[u][3] * len(units[u][2])
                        bank = wait_filled(act, ("PT", u))
                        if u >= 3:
                            act.wait_ge(pv_done, u - 2)
                        copy_out(("PT", u), probT[:, u % 3, 0:n], bank[:, 0:n])
                    if s < N_UNITS:
                        exponent(s)

            def exponent(u):
                branch, i, heads, keys = units[u]
                act.wait_ge(max_ready, u + 1)
                if u >= 3:
                    wait_filled(act, ("PT", u - 3))
                bank = psum[uses["S", u][0]]
                for n, head in enumerate(heads):
                    col = stat(branch, i, head)
                    cols = slice(keys * n, keys * n + keys)
                    src = prob[:, u % 3, cols] if branch == "A" else bank[:, cols]
                    ins = nc.scalar.activation(prob[:, u % 3, cols], src, ACT.Exp, bias=negmax[:, col:col + 1],
                                               scale=score_scale(branch, i, [head]), accum_out=rowsum[:, col:col + 1])
                ins.then_inc(exp_ready if branch == "A" else free(("S", u)), 1)

            for c in range(N_CHUNKS + LEAD_HI):
                if c < KC:
                    x_hi(c)
                if c == 0:
                    act.wait_ge(gain_in, 16)
                if c < N_CHUNKS:
                    split_hi(c)
                if c == LEAD_HI:
                    act.wait_ge(consts_ready, 1)
                for event in at.get(c - LEAD_HI, []):
                    scalar_event(event)

        @block.vector
        def _(dve):
            own = [0]

            def mark(ins):
                own[0] += 1
                ins.then_inc(dve_own, 1)
                return own[0]

            def then(ins):
                dve.wait_ge(dve_own, mark(ins))

            def low_part(dst, src, hi):
                return nc.vector.tensor_tensor(dst, src, hi.bitcast(F32), ALU.subtract)

            def split_lo(c):
                cols = GROUPS[c // KC][2]
                dve.wait_ge(hi_ready, c + 1)
                dst, src = w_lo[:, c % N_SPLIT, 0:cols], w_raw[:, c % N_RAW, 0:cols]
                hi = w_hi[:, c % N_SPLIT, 0:cols]
                if gain_of(c) is None:
                    low_part(dst, src, hi).then_inc(lo_ready, 1)
                else:
                    nc.vector.scalar_tensor_tensor(dst, src, gain_of(c), hi.bitcast(F32), ALU.mult, ALU.subtract)\
                        .then_inc(lo_ready, 1)

            def x_lo(k):
                dve.wait_ge(xT_hi_ready, k + 1)
                low_part(hT_lo[:, k, :], xT_raw[:, k, :], hT_hi[:, k, :]).then_inc(xT_lo_ready, 1)

            q_row, k_row = gain[:, GAIN_COLS:GAIN_COLS + BD], gain[:, GAIN_COLS + BD:GAIN_COLS + 2 * BD]

            def make_constants():
                dve.wait_ge(gain_in, 16)
                dve.wait_ge(tab_in, 16)
                nc.vector.tensor_tensor(kgain[:, 0:1], gain[:, G_QA:G_QA + 1], gain[:, G_KA:G_KA + 1], ALU.mult)
                nc.vector.tensor_tensor(kgain[:, 1:2], gain[:, G_QM:G_QM + 1], gain[:, G_KM:G_KM + 1], ALU.mult)
                nc.vector.tensor_tensor(qb_row[:, 0:HD], q_row[:, 0:HD], k_row[:, 0:HD], ALU.mult)
                nc.vector.tensor_copy(qb_row[:, HD:BD], q_row[:, HD:BD]).then_inc(consts_ready, 1)
                dve.wait_ge(consts_ready, 1)

            topk_mark = [0] * 3

            def rotate(part, tmp, cos, sin, whole):
                n = ROPE // 2
                nc.vector.tensor_tensor(tmp[0], part, cos, ALU.mult)
                nc.vector.tensor_tensor(tmp[1][:, :, 0:n], part[:, :, n:ROPE], sin[:, :, 0:n], ALU.mult)
                then(nc.vector.tensor_tensor(tmp[1][:, :, n:ROPE], part[:, :, 0:n], sin[:, :, n:ROPE], ALU.mult))
                return nc.vector.tensor_tensor(whole, tmp[0], tmp[1], ALU.add)

            def vector_event(event):
                kind = event[0]
                if kind == "mem_norm":
                    for n in range(4):
                        dve.wait_ge(mT_hi_ready, n + 1)
                        ks = slice(2 * n, 2 * n + 2)
                        low_part(mT_lo[:, ks, :], memT_raw[:, ks, :], mT_hi[:, ks, :]).then_inc(mT_lo_ready, 1)
                if event == ("evac", "idx"):
                    for h in range(IH):
                        key = ("acc", "idx", h // 2)
                        part = slice(HD * (h % 2), HD * (h % 2) + HD)
                        other = slice(HD - part.start, P - part.start)
                        bank = wait_filled(dve, key)
                        dve.wait_ge(idx_hi_ready, 2 * (h // 2) + 2)
                        ins = low_part(qidx_parts[other, h, :], bank[part, :], qidx_parts[part, h, :])
                        if h % 2:
                            ins.then_inc(free(key), 1)
                if kind == "kidx_T":
                    bank = wait_filled(dve, event)
                    dve.wait_ge(idx_hi_ready, IH + 1)
                    low_part(kidx_lo[:, :], bank[:, :], kidx_hi[:, :]).then_inc(free(event), 1)
                if kind == "evac" and event[1].startswith("out"):
                    side = int(event[1][3:])
                    dve.wait_ge(x_in, 32)
                    for t in range(NT):
                        key = ("acc", event[1], t)
                        dst = x_res[:, t, 512 * side:512 * side + 512]
                        nc.vector.tensor_tensor(dst, wait_filled(dve, key)[:, :], dst, ALU.add).then_inc(free(key), 1)
                if kind == "rel":
                    u = event[1]
                    i, h = 1 + u // IH, u % IH
                    keys = P * (i + 1)
                    s = score[:, score_at(i):score_at(i) + keys]
                    wait_copied(dve, event)
                    if h == 0:
                        nc.vector.tensor_scalar(s, relu_ring[:, u % N_RELU, 0:keys], w_idx[:, i, 0:1], None, ALU.mult)\
                            .then_inc(relu_used, 1)
                    else:
                        dve.wait_ge(relu_used, u)
                        nc.vector.scalar_tensor_tensor(s, relu_ring[:, u % N_RELU, 0:keys], w_idx[:, i, h:h + 1], s,
                                                       ALU.mult, ALU.add).then_inc(relu_used, 1)
                    if h == IH - 1:
                        dve.wait_ge(relu_used, u + 1)
                        topk_mark[i - 1] = mark(nc.vector.memset(s[0:64, keys - 64:keys], INADMISSIBLE))
                if kind == "topk":
                    b = event[1] - 1
                    s = score[:, score_at(b + 1):score_at(b + 2)]
                    dve.wait_ge(dve_own, topk_mark[b])
                    then(nc.vector.max(top8[:, b, :], s))
                    topk_mark[b] = mark(nc.vector.match_replace(s, top8[:, b, :], s, MARK))
                if kind == "krope":
                    wait_copied(dve, ("acc", "kwz", NT - 1))
                    then(nc.vector.tensor_tensor(krot_tmp[:, 0, :, :], krope[:, :, :], krope[:, :, :], ALU.mult))
                    nc.vector.tensor_reduce(krss[:, :], krot_tmp[:, 0, :, :], AX.X, ALU.add)
                    row = k_row[:, HD:BD].unsqueeze(1).broadcast_to([P, NT, ROPE])
                    then(nc.vector.tensor_tensor(krot[:, :, :], krope[:, :, :], row, ALU.mult))
                    rotate(krot[:, :, :], (krot_tmp[:, 0, :, :], krot_tmp[:, 1, :, :]),
                           rope_tab[:, :, 0:ROPE], rope_tab[:, :, ROPE:], krot[:, :, :]).then_inc(krot_ready, 1)
                if kind == "b_proj":
                    t = event[1]
                    dve.wait_ge(squares_ready, t + 1)
                    nc.vector.tensor_reduce(bss[:, t, 0:BH], head_sq[:, 0:576].rearrange("p (h d) -> p h d", h=BH),
                                            AX.X, ALU.add)
                    nc.vector.tensor_reduce(bss[:, t, BH:], head_sq[:, 576:960].rearrange("p (h d) -> p h d", h=BH),
                                            AX.X, ALU.add).then_inc(sums_ready, 1)
                    dve.wait_ge(sums_ready, sums.index(event) + 1)
                    dve.wait_ge(b_scalar_done, t + 1)
                    if t:
                        wait_filled(dve, ("b_T", t - 1, 2))
                    for j in range(2):
                        key = (kind, t, j)
                        nc.vector.tensor_tensor(
                            q_nat[:, 3 * j:3 * j + 3, :], wait_filled(dve, key)[:, 0:288].rearrange("p (h d) -> p h d", h=3),
                            qb_row[:, :].unsqueeze(1).broadcast_to([P, 3, BD]), ALU.mult).then_inc(free(key), 1)
                    wait_copied(dve, (kind, t, 1))
                    cos = rope_tab[:, t, 0:ROPE].unsqueeze(1).broadcast_to([P, BH, ROPE])
                    sin = rope_tab[:, t, ROPE:].unsqueeze(1).broadcast_to([P, BH, ROPE])
                    rotate(q_nat[:, :, HD:BD], (rope_tmp[:, 0, :, :], rope_tmp[:, 1, :, :]), cos, sin,
                           q_nat[:, :, HD:BD])
                if kind == "b_scale":
                    t = event[1]
                    wait_root(dve, ("b_proj", t))
                    for j in range(2):
                        key = ("b_proj", t, 2 + j)
                        r = br[:, t, 2 * BH + 3 * j:2 * BH + 3 * j + 3].unsqueeze(2).broadcast_to([P, 3, HD])
                        nc.vector.tensor_tensor(
                            k_nat[:, 3 * j:3 * j + 3, 0:HD],
                            wait_filled(dve, key)[:, 0:384].rearrange("p (h c) -> p h c", h=3)[:, :, 0:HD],
                            r, ALU.mult).then_inc(free(key), 1)
                    dve.wait_ge(krot_ready, 1)
                    nc.vector.tensor_tensor(k_nat[:, :, HD:BD], krot[:, t, :].unsqueeze(1).broadcast_to([P, BH, ROPE]),
                                            br[:, t, BH:2 * BH].unsqueeze(2).broadcast_to([P, BH, ROPE]), ALU.mult)\
                        .then_inc(b_nat_ready, 1)
                if kind == "km_norm":
                    dve.wait_ge(pool_squares, squared.index(("km",)) + 1)
                    nc.vector.tensor_reduce(kss[:, NT * AH:], kvm_sq[:, :, :].rearrange("p m (h d) -> p (m h) d", h=MH),
                                            AX.X, ALU.add).then_inc(sums_ready, 1)
                if kind == "km_scale":
                    wait_root(dve, ("km_norm",))
                    wait_copied(dve, ("acc", "mem", 1))
                    for m in range(2):
                        k = kvm[:, m, 0:MH * HD].rearrange("p (h d) -> p h d", h=MH)
                        r = kr[:, NT * AH + MH * m:NT * AH + MH * m + MH].unsqueeze(2).broadcast_to([P, MH, HD])
                        ins = nc.vector.tensor_tensor(k, k, r, ALU.mult)
                    ins.then_inc(km_ready, 1)
                if kind == "ka_norm":
                    for t in (2, 3):
                        ins = ka_sums(t)
                    ins.then_inc(sums_ready, 1)
                if kind == "ka_sums":
                    for t in (0, 1):
                        ka_sums(t)
                if kind == "ka_scale":
                    wait_root(dve, ("ka_norm",))
                    wait_copied(dve, ("acc", "ka", NT - 1))
                    k = ka_nat[:, :, :].rearrange("p t (h d) -> p (t h) d", h=AH)
                    nc.vector.tensor_tensor(k, k, kr[:, 0:NT * AH].unsqueeze(2).broadcast_to([P, NT * AH, HD]),
                                            ALU.mult).then_inc(ka_ready, 1)
                if kind == "c_sum":
                    wait_root(dve, ("x_norm",))
                    nc.vector.tensor_tensor(css[:, :, :],
                                            wait_filled(dve, event)[:, 0:2 * NT].rearrange("p (t a) -> p t a", t=NT),
                                            rx2[:, :].unsqueeze(2).broadcast_to([P, NT, 2]), ALU.mult)\
                        .then_inc(free(event), 1)
                if kind in ("qa_sum", "qm_sum"):
                    lo, heads = (0, AH) if kind == "qa_sum" else (NT * AH, MH)
                    n = NT * heads
                    nc.vector.tensor_tensor(qms[:, lo:lo + n].rearrange("p (t h) -> p t h", t=NT),
                                            wait_filled(dve, event)[:, 0:n].rearrange("p (t h) -> p t h", t=NT),
                                            rx2[:, :].unsqueeze(2).broadcast_to([P, NT, heads]), ALU.mult)\
                        .then_inc(free(event), 1)
                if kind == "distances":
                    i = event[1]
                    s = score[:, score_at(i):score_at(i + 1)]
                    if i == 0:
                        dve.wait_ge(tab_in, 16)
                        then(nc.vector.tensor_copy(s, ndist[:, 512 - P:512]))
                        nc.vector.memset(s[0:64, P - 64:P], NEG).then_inc(dist_ready, 1)
                    else:
                        dve.wait_ge(dve_own, topk_mark[i - 1])
                        then(nc.vector.tensor_scalar(s, s, MARKED_BELOW, NEG, ALU.is_gt, ALU.mult))
                        nc.vector.tensor_tensor(s, s, ndist[:, 512 - P * (i + 1):512], ALU.add).then_inc(dist_ready, 1)
                if kind == "step":
                    s = event[1]
                    if s - TURN_Y in last_unit:
                        branch, i = last_unit[s - TURN_Y]
                        first, n = y_cols[branch]
                        key = ("y_T", branch, i)
                        bank = wait_filled(dve, key)
                        dve.wait_ge(yT_hi_ready, y_number[branch, i] + 1)
                        hi, lo = yT[branch]
                        low_part(lo[:, :, tile(i)], bank[:, 0:P * n].rearrange("p (k n) -> p k n", k=n),
                                 hi[:, :, tile(i)]).then_inc(free(key), 1)
                    if s < N_UNITS:
                        row_max(s)
                    if s - SCALE_Y in last_unit:
                        scale_y(s - SCALE_Y)

            def ka_sums(t):
                dve.wait_ge(pool_squares, squared.index(("ka", t)) + 1)
                return nc.vector.tensor_reduce(kss[:, AH * t:AH * t + AH],
                                               ka_sq[:, t, :].rearrange("p (h d) -> p h d", h=AH), AX.X, ALU.add)

            def row_max(u):
                branch, i, heads, keys = units[u]
                bank = wait_filled(dve, ("S", u))
                if first_unit.get(u, ("", 1))[1] == 0:
                    wait_root(dve, {"B": ("b_proj", 0), "M": ("qm_sum",), "A": ("qa_sum",)}[branch])
                cols = stats_of(branch, i, heads)
                if branch == "A":
                    n = a_units.index(u)
                    dve.wait_ge(bias_ready, n + 1)
                    wait_filled(dve, ("PT", u - 3))
                    for m, h in enumerate(heads):
                        col = stat(branch, i, h)
                        part = slice(keys * m, keys * m + keys)
                        at_head = n % 2 * 512 + keys * m
                        ins = nc.vector.tensor_tensor_reduce(
                            out=prob[:, u % 3, part], in0=bank[:, part], in1=bias_ring[:, at_head:at_head + keys],
                            scale=1.0, scalar=-3.4e38, op0=ALU.add, op1=ALU.max, accum_out=rowmax[:, col:col + 1])
                    ins.then_inc(free(("S", u)), 1)
                    wait_copied(dve, ("S", u))
                else:
                    by_head = bank[:, 0:keys * len(heads)].rearrange("p (h n) -> p h n", h=len(heads))
                    if branch == "B":
                        then(nc.vector.memset(by_head[0:64, :, keys - 64:keys], NEG))
                    then(nc.vector.tensor_reduce(rowmax[:, cols], by_head, AX.X, ALU.max))
                nc.vector.scalar_tensor_tensor(negmax[:, cols], rowmax[:, cols], -1.0, score_scale(branch, i, heads),
                                               ALU.mult, ALU.mult).then_inc(max_ready, 1)

            def scale_y(u):
                branch, i = last_unit[u]
                first, n = y_cols[branch]
                heads = 2 * n
                dve.wait_ge(pv_done, u + 1)
                dve.wait_ge(gate_scaled, y_number[branch, i] + 1)
                y = gates[:, i, P * first:P * (first + n)].rearrange("p (h d) -> p h d", h=heads)
                bank = psum[uses["O", branch, i][0]]
                nc.vector.tensor_tensor(y, bank[:, 0:HD * heads].rearrange("p (h d) -> p h d", h=heads), y,
                                        ALU.mult).then_inc(free(("O", branch, i)), 1)

            for c in range(N_CHUNKS + LEAD):
                if c < KC:
                    x_lo(c)
                if c < N_CHUNKS:
                    split_lo(c)
                if c == 0:
                    make_constants()
                for event in at.get(c - LEAD, []):
                    vector_event(event)

        @block.tensor
        def _(pe):
            def transpose(dst, src):
                return nc.tensor.transpose(dst, src, ident)

            def project(c, halfway):
                g, k = divmod(c, KC)
                name, _, cols, transposed = GROUPS[g]
                s = c % N_SPLIT
                hi_w, lo_w = w_hi[:, s, 0:cols], w_lo[:, s, 0:cols]
                hi_t, lo_t = (mT_hi, mT_lo) if name == "mem" else (hT_hi, hT_lo)
                row = k
                if name == "idx":
                    pe.wait_ge(xT_hi_ready, k + 1)
                    pe.wait_ge(xT_lo_ready, k + 1)
                if name == "mem":
                    pe.wait_ge(mT_lo_ready, k // 2 + 1)
                if name.startswith("out"):
                    branch, first = [(b, first) for b, (first, n) in y_cols.items()
                                     if first <= OUT_ORDER[k] < first + n][0]
                    hi_t, lo_t = yT[branch]
                    row = OUT_ORDER[k] - first
                    if name == "out0" and row == 0:
                        wait_copied(pe, ("y_T", branch, NT - 1))
                pe.wait_ge(hi_ready, c + 1)
                pe.wait_ge(lo_ready, c + 1)
                for j in range(banks_of(name)):
                    key = ("acc", name, j)
                    bank = psum[uses[key][0]]
                    if k == 0:
                        wait_free(pe, key)
                    if transposed:
                        dst = bank[:, :]
                        passes = [(hi_w[:, tile(j)], hi_t[:, row, :]), (hi_w[:, tile(j)], lo_t[:, row, :]),
                                  (lo_w[:, tile(j)], hi_t[:, row, :])]
                    else:
                        dst = bank[:, 0:cols]
                        passes = [(hi_t[:, row, tile(j)], hi_w), (hi_t[:, row, tile(j)], lo_w),
                                  (lo_t[:, row, tile(j)], hi_w)]
                    for n, (stationary, moving) in enumerate(passes):
                        ins = nc.tensor.matmul(dst, stationary, moving, start=(k == 0 and n == 0),
                                               stop=(k == KC - 1 and n == 2))
                    if k == KC - 1:
                        ins.then_inc(filled(key), 1)
                    elif j == banks_of(name) - 1:
                        ins.then_inc(chunk_used, 1)
                    if j == 1:
                        for event in halfway:
                            tensor_event(event)

            def tensor_event(event):
                kind = event[0]
                if kind == "kidx_T":
                    pe.wait_ge(tab_in, 16)
                    pe.wait_ge(kidx_ready, NT)
                    bank = wait_free(pe, event)
                    for t in range(NT):
                        ins = transpose(bank[:, tile(t)], kidx_nat[:, t, :])
                    ins.then_inc(filled(event), 1)
                if kind == "rel":
                    u = event[1]
                    i, h = 1 + u // IH, u % IH
                    half_ = slice(HD * (h % 2), HD * (h % 2) + HD)
                    keys = P * (i + 1)
                    if u == 0:
                        wait_copied(pe, ("kidx_T",))
                        wait_copied(pe, ("acc", "idx", 3))
                    bank = wait_free(pe, event)
                    q = qidx_parts[:, h, tile(i)]
                    nc.tensor.matmul(bank[:, 0:keys], q, kidx_hi[:, 0:keys], start=True, stop=False)
                    nc.tensor.matmul(bank[:, 0:keys], q, kidx_lo[:, 0:keys], start=False, stop=True)\
                        .then_inc(filled(event), 1)
                if kind == "c_sum":
                    wait_copied(pe, ("acc", "c", 2))
                    bank = wait_free(pe, event)
                    for t in range(NT):
                        for j in range(3):
                            col = 2 * t + j // 2
                            ins = nc.tensor.matmul(bank[:, col:col + 1], qsT[:, j, tile(t)], ones1,
                                                   start=(j != 1), stop=(j != 0))
                    ins.then_inc(filled(event), 1)
                if kind == "b_proj":
                    t = event[1]
                    if t == 0:
                        pe.wait_ge(uw_in, 32)
                    for j in range(2):
                        key = (kind, t, j)
                        bank = wait_free(pe, key)
                        for k in range(2):
                            ins = nc.tensor.matmul(bank[:, 0:288], cT[:, k, tile(t)], uq[:, k, 288 * j:288 * j + 288],
                                                   start=(k == 0), stop=(k == 1))
                        ins.then_inc(filled(key), 1)
                    for j in range(2):
                        key = (kind, t, 2 + j)
                        bank = wait_free(pe, key)
                        nc.tensor.matmul(bank[:, 0:384], cT[:, 2, tile(t)], ukv[:, 384 * j:384 * j + 384],
                                         start=True, stop=True).then_inc(filled(key), 1)
                if kind == "b_T":
                    t = event[1]
                    pe.wait_ge(b_nat_ready, t + 1)
                    for j in range(3):
                        key = (kind, t, j)
                        bank = wait_free(pe, key)
                        for n in range(4):
                            m = 4 * j + n
                            src = q_nat[:, m, :] if m < BH else k_nat[:, m - BH, :]
                            ins = transpose(bank[0:BD, tile(n)], src)
                        ins.then_inc(filled(key), 1)
                if kind == "km_T":
                    pe.wait_ge(km_ready, 1)
                    bank = wait_free(pe, event)
                    for j in range(2):
                        for m in range(2):
                            ins = transpose(bank[:, tile(2 * j + m)], kvm[:, m, P * j:P * j + P])
                    ins.then_inc(filled(event), 1)
                if kind == "ka_T":
                    pe.wait_ge(ka_ready, 1)
                    for j in range(3):
                        bank = wait_free(pe, (kind, j))
                        for t in range(NT):
                            ins = transpose(bank[:, tile(t)], ka_nat[:, t, P * j:P * j + P])
                        ins.then_inc(filled((kind, j)), 1)
                if kind in ("qa_sum", "qm_sum"):
                    name, tiles = ("qa", 3) if kind == "qa_sum" else ("qm", 2)
                    pe.wait_ge(pool_squares, squared.index((name, tiles - 1)) + 1)
                    bank = wait_free(pe, event)
                    for t in range(NT):
                        for j in range(tiles):
                            col = 2 * tiles * t + 2 * j
                            ins = nc.tensor.matmul(bank[:, col:col + 2], qsT[:, j, tile(t)], ones2,
                                                   start=True, stop=True)
                    ins.then_inc(filled(event), 1)

                if kind == "step":
                    s = event[1]
                    turns_y = s - TURN_Y in last_unit
                    if turns_y:
                        branch, i = last_unit[s - TURN_Y]
                        first, n = y_cols[branch]
                        wait_copied(pe, ("O", branch, i))
                        bank = wait_free(pe, ("y_T", branch, i))
                        for m in range(n):
                            ins = transpose(bank[:, tile(m)], gates[:, i, P * (first + m):P * (first + m) + P])
                        ins.then_inc(filled(("y_T", branch, i)), 1)
                    if 0 <= s - TRANSPOSE < N_UNITS and not turns_y:
                        transpose_probs(s - TRANSPOSE)
                    if s < N_UNITS:
                        scores(s)
                    if 0 <= s - WEIGH < N_UNITS:
                        weigh_values(s - WEIGH)
                    if 0 <= s - TRANSPOSE < N_UNITS and turns_y:
                        transpose_probs(s - TRANSPOSE)

            def scores(u):
                branch, i, heads, keys = units[u]
                if u in first_unit:
                    if branch == "B":
                        wait_copied(pe, ("b_T", i, 2))
                    if branch == "M" and i == 0:
                        wait_copied(pe, ("acc", "qm", 1))
                        wait_copied(pe, ("km_T",))
                    if branch == "A" and i == 0:
                        wait_copied(pe, ("acc", "qa", 2))
                        wait_copied(pe, ("ka_T", 2))
                bank = wait_free(pe, ("S", u))
                for n, head in enumerate(heads):
                    half_ = slice(HD * (head % 2), HD * (head % 2) + HD)
                    if branch == "B":
                        q, k = qbT[0:BD, head, tile(i)], kbT[0:BD, head, 0:keys]
                    if branch == "M":
                        q, k = qmT[half_, head // 2, tile(i)], kmT[half_, head // 2, :]
                    if branch == "A":
                        q, k = qaT[half_, head // 2, tile(i)], kaT[half_, head // 2, 0:keys]
                    ins = nc.tensor.matmul(bank[:, keys * n:keys * n + keys], q, k, start=True, stop=True)
                ins.then_inc(filled(("S", u)), 1)

            def transpose_probs(u):
                branch, _, heads, keys = units[u]
                if branch == "A":
                    pe.wait_ge(exp_ready, a_units.index(u) + 1)
                else:
                    wait_copied(pe, ("S", u))
                bank = wait_free(pe, ("PT", u))
                for n in range(keys * len(heads) // P):
                    ins = transpose(bank[:, tile(n)], prob[:, u % 3, tile(n)])
                ins.then_inc(filled(("PT", u)), 1)

            def weigh_values(u):
                branch, i, heads, keys = units[u]
                wait_copied(pe, ("PT", u))
                if branch == "A" and u in first_unit:
                    wait_copied(pe, ("acc", "va", i))
                if u in first_unit:
                    wait_free(pe, ("O", branch, i))
                bank = psum[uses["O", branch, i][0]]
                tiles = keys // P
                for n, head in enumerate(heads):
                    for m in range(tiles):
                        v = {"A": va, "B": vb, "M": kvm}[branch]
                        col = HD * head + (MH * HD if branch == "M" else 0)
                        ins = nc.tensor.matmul(bank[:, HD * head:HD * head + HD], probT[:, u % 3, tile(tiles * n + m)],
                                               v[:, m, col:col + HD], start=(m == 0), stop=(m == tiles - 1))
                ins.then_inc(pv_done, 1)

            for c in range(N_CHUNKS):
                first_half, second_half = [], at[c]
                if c >= TWO_STEPS_FROM:
                    first_half, second_half = at[c][:1], at[c][1:]
                project(c, first_half)
                for event in second_half:
                    tensor_event(event)


def kernel(**inputs):
    import numpy as np
    import concourse.bacc as bacc
    from concourse.bass_utils import run_bass_kernel_spmd

    g = {name: np.asarray(inputs[name])[0] for name in
         ("g_in", "g_mem", "g_cq", "g_ckv", "g_qa", "g_ka", "g_qm", "g_km", "g_qb", "g_kb")}
    columns = [g["g_in"].reshape(KC, P).T, g["g_mem"].reshape(KC, P).T, g["g_cq"].reshape(2, P).T,
               g["g_ckv"].reshape(1, P).T]
    columns += [np.tile(g[name], 2)[:, None] for name in ("g_qa", "g_ka", "g_qm", "g_km")]
    columns += [np.tile(g[name][None, :], (P, 1)) for name in ("g_qb", "g_kb")]
    arrays = {
        "x": np.ascontiguousarray(inputs["x"])[0], "xT": np.ascontiguousarray(np.asarray(inputs["x"])[0].T),
        "mem": np.ascontiguousarray(inputs["mem"])[0],
        "memT": np.ascontiguousarray(np.asarray(inputs["mem"])[0].T),
        **{name: np.ascontiguousarray(inputs[name])[0] for name in
           ("w_in", "w_uq", "w_ukv", "w_mk", "w_mv", "w_out")},
        "gains": np.ascontiguousarray(np.concatenate(columns, axis=1)),
        "tables": shape_tables(),
    }
    nc = bacc.Bacc("TRN2", target_bir_lowering=False, num_devices=1)
    args = [nc.dram_tensor(f"in_{name}", a.shape, mybir.dt.from_np(a.dtype), kind="ExternalInput").ap()
            for name, a in arrays.items()]
    args.append(nc.dram_tensor("out_y", (SEQ, DM), F32, kind="ExternalOutput").ap())
    build_layer(nc, *args)
    r = run_bass_kernel_spmd(nc, [{f"in_{name}": a for name, a in arrays.items()}], core_ids=[0])
    return r.results[0]["out_y"].reshape(1, SEQ, DM)


def shape_tables():
    import numpy as np

    f = np.float32
    n = ROPE // 2
    inv = f(1.0) / (f(10000.0) ** (np.arange(n, dtype=f) / f(n)))
    ang = np.arange(SEQ, dtype=f)[:, None] * inv[None, :]
    cos, sin = np.cos(ang), np.sin(ang)
    rope = np.concatenate([cos, cos, -sin, sin], axis=1).reshape(NT, P, 4 * n).transpose(1, 0, 2).reshape(P, -1)
    ones = np.ones((P, 3), f)
    ones[:, :2] = 0
    ones[:P // 2, 0] = 1
    ones[P // 2:, 1] = 1
    dist = -np.abs((SEQ - P + np.arange(P))[:, None] - np.arange(SEQ)[None, :]).astype(f)
    slopes = (f(2.0) ** (f(-8.0) * np.arange(1, AH + 1, dtype=f) / f(AH))) / f(A_SCALE)
    return np.ascontiguousarray(np.concatenate(
        [np.eye(P, dtype=f), rope, ones, dist, np.tile(slopes, (P, NT))], axis=1).astype(f))
```

```python
import concourse.bass as bass
from concourse import mybir
from contextlib import ExitStack

F32 = mybir.dt.float32
F32R = mybir.dt.float32r
ALU = mybir.AluOpType
ACT = mybir.ActivationFunctionType
AX = mybir.AxisListType

P = 128
SEQ, DM, NMEM = 512, 1024, 256
NT, KC = SEQ // P, DM // P
EPS = 1e-6
HD = 64
AH, BH, MH, IH = 6, 6, 4, 8
BD, ROPE = 96, 32
QL, KVL = 256, 128
TOPK = 128
W_WIDTH = 512
N_RAW, N_SPLIT = 6, 6
N_RELU = 4
LOADS = {"tab": 3, "x_first": 7, "x_rest": 9, "memT": 11, "u": 13, "mem": 15, "mask": 34}
EARLY = {"x_norm": 9, "mem_split": 11, "u_split": 12, "mem_norm": 13}
WARM_UP = (512, 512, 128)
KM_T, KA_T = 18, 6
LEAD_HI, LEAD = 4, 3
MARK, INADMISSIBLE, MARKED_BELOW = -3.4e38, -3.0e38, -3.2e38
NEG = -1.0e30
A_SCALE, B_SCALE, M_SCALE = HD ** -0.5, BD ** -0.5, HD ** -0.5

G_IN, G_MEM, G_CQ, G_CKV, G_QA, G_KA, G_QM, G_KM, GAIN_COLS = 0, 8, 16, 18, 19, 20, 21, 22, 23

GROUPS = [
    ("idx", 1152, 512, True), ("kwz", 1664, 488, False), ("c", 2120, 384, True),
    ("mem", 0, 512, False), ("zb", 2536, 384, False), ("ka", 384, 384, False), ("qa", 0, 384, True),
    ("va", 768, 384, False), ("qm", 2920, 256, True), ("zm", 3176, 256, False),
    ("out0", 0, 512, False), ("out1", 512, 512, False),
]
K_ROPE = 2504
NAMES = [g[0] for g in GROUPS]
N_IN_CHUNKS = KC * NAMES.index("out0")
N_CHUNKS = KC * len(GROUPS)
OUT_ORDER = [3, 4, 5, 0, 1, 2, 6, 7]


def last_chunk(name):
    return KC * NAMES.index(name) + KC - 1


def attention_units():
    units = []
    for i, heads in enumerate([[(0, 1, 2), (3, 4, 5)], [(0, 1), (2, 3), (4, 5)]] + 2 * [[(h,) for h in range(6)]]):
        units += [("B", i, hs, P * (i + 1)) for hs in heads]
    for i, heads in enumerate([[(0, 2, 4), (1, 3, 5)], [(0, 2), (1, 3), (4,), (5,)]] + 2 * [[(h,) for h in range(6)]]):
        units += [("A", i, hs, P * (i + 1)) for hs in heads]
    units += [("M", i, hs, NMEM) for i in range(NT) for hs in [(0, 2), (1, 3)]]
    return units


N_UNITS = len(attention_units())
TOPK_FIRST = 26
TOPK_TWO = (30, 31, 33, 34, 37, 38, 41, 42, 45, 46)
FIRST_STEP = 44
TWO_STEPS_FROM = 80
TRANSPOSE, WEIGH, SCALE_GATE, SCALE_Y, TURN_Y = 2, 3, 1, 3, 5
N_STEPS = N_UNITS + TURN_Y


def schedule():
    at = {c: [] for c in range(N_CHUNKS)}
    for event, c in EARLY.items():
        at[c].append((event,))
    for name in NAMES:
        at[last_chunk(name)].append(("evac", name))
    at[last_chunk("kwz") + 1].append(("krope",))
    at[last_chunk("kwz") + 2].append(("kidx_T",))
    for u in range(3 * IH):
        at[last_chunk("kwz") + 4 + u // 4].append(("rel", u))
    at[last_chunk("c") + 2].append(("c_sum",))
    for t in range(NT):
        at[last_chunk("c") + 5 + 4 * t].append(("b_proj", t))
        at[last_chunk("c") + 7 + 4 * t].append(("b_scale", t))
        at[last_chunk("c") + 9 + 4 * t].append(("b_T", t))
    at[last_chunk("mem") + 2].append(("km_norm",))
    at[last_chunk("mem") + KM_T].append(("km_T",))
    at[last_chunk("ka") + 1].append(("ka_sums",))
    at[last_chunk("ka") + 2].append(("ka_norm",))
    for j in range(3):
        at[last_chunk("ka") + KA_T + j].append(("ka_T", j))
    at[last_chunk("qa") + 2].append(("qa_sum_first",))
    at[last_chunk("qa") + 3].append(("qa_sum",))
    at[last_chunk("qm") + 2].append(("qm_sum_first",))
    at[last_chunk("qm") + 3].append(("qm_sum",))
    for s in range(N_STEPS):
        c = FIRST_STEP + s
        if c >= TWO_STEPS_FROM:
            c = TWO_STEPS_FROM + (c - TWO_STEPS_FROM) // 2
        at[c].append(("step", s))
    at[last_chunk("c") + 1].append(("distances", 0))
    left = {i: TOPK // 8 for i in range(1, NT)}
    for c in range(TOPK_FIRST, N_IN_CHUNKS):
        kinds = [e[0] for e in at[c]]
        n = 0 if "b_proj" in kinds or "ka_norm" in kinds else 1 + (c in TOPK_TWO)
        for second in range(n):
            tiles = [i for i in left if left[i] and c >= TOPK_FIRST + 2 * (i - 1)]
            if not tiles:
                break
            i = tiles[(c + second) % min(2, len(tiles))]
            at[c].append(("topk", i))
            left[i] -= 1
            if not left[i]:
                at[c].append(("distances", i))
    assert not any(left.values())
    return at


def score_at(i):
    return P * i * (i + 1) // 2


def build_layer(nc, x, xT, mem, memT, w_in, w_uq, w_ukv, w_mk, w_mv, w_out, gains, tables, chunk_mask, out):
    at = schedule()
    units = attention_units()
    ctx = ExitStack()
    with ctx:
        base = [nc.sbuf_base + 31 & ~31]
        arena_bytes = nc.sbuf_usable_end - base[0] - 64
        ctx.enter_context(nc.sbuf_tensor("arena", [P, arena_bytes], mybir.dt.uint8))

        def place(name, shape, dt=F32, over=None, skip=0):
            size = 4
            for n in shape:
                size *= n
            if over is None:
                offset = base[0]
                base[0] += (size + 31) // 32 * 32
            else:
                offset = over + skip
            assert base[0] <= nc.sbuf_usable_end, (name, base[0])
            return nc.alloc_sbuf_tensor_at(name, [P] + list(shape), dt, offset=offset), offset

        x_nat, at_x = place("x_nat", [NT, DM])
        hT_hi, at_hT = place("hT_hi", [KC, SEQ], F32R)
        hT_lo, at_hT_lo = place("hT_lo", [KC, SEQ], F32R)
        x_res, _ = place("x_res", [NT, DM], F32, at_hT)
        w_raw, _ = place("w_raw", [N_RAW, W_WIDTH])
        w_hi, _ = place("w_hi", [N_SPLIT, W_WIDTH], F32R)
        w_lo, _ = place("w_lo", [N_SPLIT, W_WIDTH], F32R)
        gates, at_gates = place("gates", [NT, DM])
        xT_raw, _ = place("xT_raw", [KC, SEQ], F32, at_gates)
        qbT, at_qb = place("qbT", [BH, SEQ])
        qidx_parts, _ = place("qidx_parts", [IH, SEQ], F32R, at_qb)
        kidx_hi, _ = place("kidx_hi", [SEQ], F32R, at_qb, 4 * IH * SEQ)
        kidx_lo, _ = place("kidx_lo", [SEQ], F32R, at_qb, 4 * (IH + 1) * SEQ)
        yT = {}
        for branch, n, over in [("B", 3, at_x), ("A", 3, at_qb), ("M", 2, at_hT_lo)]:
            yT[branch] = [place(f"y{branch}T_{part}", [n, SEQ], F32R, over, 4 * n * SEQ * m)[0]
                          for m, part in enumerate(["hi", "lo"])]
        kbT, at_kb = place("kbT", [BH, SEQ])
        memT_raw, _ = place("memT_raw", [KC, NMEM], F32, at_qb, 4 * (IH + 2) * SEQ)
        vb, _ = place("vb", [NT, BH * HD])
        va, at_va = place("va", [NT, AH * HD])
        qaT, _ = place("qaT", [3, SEQ])
        kaT, _ = place("kaT", [3, SEQ])
        ka_nat, _ = place("ka_nat", [NT, AH * HD], F32, at_va)
        mT_hi, _ = place("mT_hi", [KC, NMEM], F32R, at_va)
        mT_lo, _ = place("mT_lo", [KC, NMEM], F32R, at_va, 4 * KC * NMEM)
        qmT, _ = place("qmT", [2, SEQ])
        kmT, _ = place("kmT", [2, NMEM])
        kvm, _ = place("kvm", [2, 512])
        w_idx, _ = place("w_idx", [NT, IH])
        uq, at_uq = place("uq", [2, BH * BD])
        ukv, at_ukv = place("ukv", [BH * 2 * HD])
        uq_lo, _ = place("uq_lo", [2, BH * BD], F32R, at_uq)
        ukv_lo, _ = place("ukv_lo", [BH * 2 * HD], F32R, at_ukv)
        uq_hi, _ = place("uq_hi", [2, BH * BD], F32R, at_x, 4 * N_RELU * 512)
        ukv_hi, _ = place("ukv_hi", [BH * 2 * HD], F32R, at_x, 4 * (N_RELU * 512 + 2 * BH * BD))
        score, at_score = place("score", [score_at(NT)])
        zeros, _ = place("zeros", [512], F32, at_score)
        prob, at_prob = place("prob", [3, 512])
        probT, at_probT = place("probT", [3, 512])
        cT_hi, _ = place("cT_hi", [3, SEQ], F32R, at_prob)
        cT_lo, _ = place("cT_lo", [3, SEQ], F32R, at_probT)
        mem_nat, _ = place("mem_nat", [2, DM], F32, at_prob)
        squares, _ = place("squares", [DM], F32, at_probT, 2048)
        bias_ring, at_bias = place("bias_ring", [1152])
        relu_ring, _ = place("relu_ring", [N_RELU, 512], F32, at_x)
        kidx_nat, _ = place("kidx_nat", [NT, 2 * HD], F32, at_bias)
        q_nat, _ = place("q_nat", [BH, BD], F32, at_bias)
        k_nat, _ = place("k_nat", [BH, BD], F32, at_bias, 4 * BH * BD)
        qsT, at_c = place("qsT", [3, SEQ])
        kvm_sq, _ = place("kvm_sq", [2, MH * HD], F32, at_c)
        ka_sq, _ = place("ka_sq", [NT, AH * HD], F32, at_c)
        head_sq, at_hsq = place("head_sq", [960])
        rope_tmp, _ = place("rope_tmp", [2, BH, ROPE], F32, at_hsq)
        krope, _ = place("krope", [NT, ROPE])
        krot, _ = place("krot", [NT, ROPE])
        krot_tmp, _ = place("krot_tmp", [2, NT, ROPE], F32, at_hsq)
        gain, _ = place("gain", [GAIN_COLS + 2 * BD])
        tab, _ = place("tab", [P + 64 * NT + 3 + 512 + AH * NT])
        half, _ = place("half", [32])
        minus_one, _ = place("minus_one", [BH])
        table_load, _ = place("table_load", [1])
        kgain, _ = place("kgain", [2])
        qb_row, _ = place("qb_row", [BD])
        ssx, _ = place("ssx", [NT + 2])
        msx, _ = place("msx", [NT + 2])
        rx, _ = place("rx", [NT + 2])
        rx2, _ = place("rx2", [NT])
        irx, _ = place("irx", [NT])
        css, _ = place("css", [NT, 2])
        cr, _ = place("cr", [NT, 2])
        cr2, _ = place("cr2", [NT, 2])
        krss, _ = place("krss", [NT])
        bss, _ = place("bss", [NT, 2 * BH])
        br, _ = place("br", [NT, 3 * BH])
        kss, _ = place("kss", [NT * AH + 2 * MH])
        kr, _ = place("kr", [NT * AH + 2 * MH])
        qms, _ = place("qms", [NT * AH + NT * MH])
        qr, _ = place("qr", [NT * AH + NT * MH])
        slope_r, _ = place("slope_r", [NT * AH])
        top8, _ = place("top8", [3, 8])
        rowmax, _ = place("rowmax", [NT * 16])
        negmax, _ = place("negmax", [NT * 16])
        rowsum, _ = place("rowsum", [NT * 16])
        rowinv, _ = place("rowinv", [NT * 16])

        ident = tab[:, 0:P]
        rope_tab = tab[:, P:P + 64 * NT].rearrange("p (t c) -> p t c", t=NT)
        ones2 = tab[:, P + 64 * NT:P + 64 * NT + 2]
        ones1 = tab[:, P + 64 * NT + 2:P + 64 * NT + 3]
        ndist = tab[:, P + 64 * NT + 3:P + 64 * NT + 3 + 512]
        slopes = tab[:, P + 64 * NT + 515:P + 64 * NT + 515 + AH * NT]

        psum = [ctx.enter_context(nc.psum_tensor(f"bank{b}", [P, 512], F32)) for b in range(8)]

        uses, fills, frees = {}, [0] * 8, [0] * 8

        def take(bank, key, filled=1, freed=1):
            uses[key] = (bank, fills[bank], frees[bank])
            fills[bank] += filled
            frees[bank] += freed

        def banks_of(name):
            _, _, cols, transposed = GROUPS[NAMES.index(name)]
            return 2 if name == "mem" else cols // P if transposed else NT

        def take_banks(event):
            kind = event[0]
            if kind == "kidx_T":
                take(4, event)
            if kind == "rel":
                take(4 + event[1] % 4, event)
            if kind == "b_proj":
                for j in range(4):
                    take(4 + j, ("b_proj", event[1], j))
            if kind == "b_T":
                for j in range(3):
                    take(4 + j, ("b_T", event[1], j))
            if kind in ("km_T", "ka_T"):
                take(3, event)
            if kind in ("c_sum", "qa_sum_first", "qa_sum", "qm_sum_first", "qm_sum"):
                take(6, event)
            if kind == "step":
                s = event[1]
                if s - TURN_Y in last_unit:
                    take(6, ("y_T",) + last_unit[s - TURN_Y])
                if 0 <= s - TRANSPOSE < N_UNITS:
                    take(6, ("PT", s - TRANSPOSE))
                if s < N_UNITS:
                    take(4 + s % 2, ("S", s))
                if s - WEIGH in first_unit:
                    take(7, ("O",) + first_unit[s - WEIGH], filled=0)

        first_unit, last_unit = {}, {}
        for u, (branch, i, _, _) in enumerate(units):
            if u == 0 or units[u - 1][:2] != (branch, i):
                first_unit[u] = (branch, i)
            if u == N_UNITS - 1 or units[u + 1][:2] != (branch, i):
                last_unit[u] = (branch, i)
        y_number = {group: n for n, group in enumerate(last_unit.values())}
        for c in range(N_CHUNKS):
            if c % KC == 0:
                for j in range(banks_of(NAMES[c // KC])):
                    take(j + 4 * (NAMES[c // KC] == "kwz"), ("acc", NAMES[c // KC], j))
            for event in at[c]:
                take_banks(event)

        def sem(name):
            return ctx.enter_context(nc.semaphore(name))

        bank_filled = [sem(f"bank_filled{b}") for b in range(8)]
        bank_free = [sem(f"bank_free{b}") for b in range(8)]
        xT_in = [sem(f"xT_in{k}") for k in range(KC)]
        raw_in = [sem(f"raw_in{s}") for s in range(N_RAW)]
        x_in, mem_in, memT_in, uw_in = sem("x_in"), sem("mem_in"), sem("memT_in"), sem("uw_in")
        zeros_ready = sem("zeros_ready")
        rows_in, mask_in = sem("rows_in"), sem("mask_in")
        gain_in, tab_in, stored = sem("gain_in"), sem("tab_in"), sem("stored")
        hi_ready, lo_ready, chunk_used = sem("hi_ready"), sem("lo_ready"), sem("chunk_used")
        act_own, dve_own, pool_own = sem("act_own"), sem("dve_own"), sem("pool_own")
        sums_ready, root_ready = sem("sums_ready"), sem("root_ready")
        xT_hi_ready, xT_lo_ready = sem("xT_hi_ready"), sem("xT_lo_ready")
        mT_hi_ready, mT_lo_ready = sem("mT_hi_ready"), sem("mT_lo_ready")
        relu_used, krot_ready, km_ready, ka_ready = sem("relu_used"), sem("krot_ready"), sem("km_ready"), sem("ka_ready")
        squares_ready, b_scalar_done, b_nat_ready = sem("squares_ready"), sem("b_scalar_done"), sem("b_nat_ready")
        consts_ready, dist_ready, bias_ready = sem("consts_ready"), sem("dist_ready"), sem("bias_ready")
        max_ready, exp_ready, pv_done = sem("max_ready"), sem("exp_ready"), sem("pv_done")
        pool_squares, gate_scaled = sem("pool_squares"), sem("gate_scaled")
        u_hi_ready, u_lo_ready, c_hi_ready = sem("u_hi_ready"), sem("u_lo_ready"), sem("c_hi_ready")
        kidx_ready, idx_hi_ready = sem("kidx_ready"), sem("idx_hi_ready")
        yT_hi_ready = sem("yT_hi_ready")

        def wait_filled(eng, key):
            bank, n, _ = uses[key]
            eng.wait_ge(bank_filled[bank], n + 1)
            return psum[bank]

        def wait_copied(eng, key):
            bank, _, n = uses[key]
            eng.wait_ge(bank_free[bank], n + 1)

        def wait_free(eng, key):
            bank, _, n = uses[key]
            if n:
                eng.wait_ge(bank_free[bank], n)
            return psum[bank]

        def filled(key):
            return bank_filled[uses[key][0]]

        def free(key):
            return bank_free[uses[key][0]]

        def wait_chunk_used(eng, c):
            g, k = divmod(c, KC)
            if k == KC - 1:
                wait_filled(eng, ("acc", NAMES[g], banks_of(NAMES[g]) - 1))
            else:
                eng.wait_ge(chunk_used, (KC - 1) * g + k + 1)

        by_bank = ("c_sum", "qa_sum", "qm_sum")
        roots = []
        for c in range(N_CHUNKS):
            for e in at[c]:
                if e[0] in ("x_norm", "mem_norm", "km_norm", "ka_norm", "b_proj") + by_bank:
                    roots.append(e)
                if e[0] == "b_proj":
                    roots.append(("b_q",) + e[1:])
        sums = [e for e in roots if e[0] not in by_bank + ("b_q",)]
        squared = [("km",)] + [("ka", t) for t in range(NT)] + [("qa", j) for j in range(3)] + [("qm", j) for j in range(2)]
        selections = [e[1] for c in range(N_CHUNKS) for e in at[c] if e[0] == "distances"]
        a_units = [u for u in range(N_UNITS) if units[u][0] == "A"]

        def wait_root(eng, key):
            eng.wait_ge(root_ready, roots.index(key) + 1)

        def gain_of(c):
            g, k = divmod(c, KC)
            if NAMES[g].startswith("out"):
                return None
            col = (G_MEM if NAMES[g] == "mem" else G_IN) + k
            return gain[:, col:col + 1]

        def tile(t):
            return slice(P * t, P * t + P)

        def stat(branch, i, h):
            return i * BH + h if branch == "B" else NT * BH + i * MH + h if branch == "M" \
                else NT * (BH + MH) + i * AH + h

        def stats_of(branch, i, heads):
            step = heads[1] - heads[0] if len(heads) > 1 else 1
            return slice(stat(branch, i, heads[0]), stat(branch, i, heads[-1]) + 1, step)

        def score_scale(branch, i, heads):
            step = heads[1] - heads[0] if len(heads) > 1 else 1
            if branch == "B":
                return br[:, i, heads[0]:heads[-1] + 1:step]
            col = i * AH if branch == "A" else NT * AH + i * MH
            return qr[:, col + heads[0]:col + heads[-1] + 1:step]

        y_cols = {"A": (0, 3), "B": (3, 3), "M": (6, 2)}

        block = ctx.enter_context(nc.Block())

        @block.sync
        def _(sp):
            xv = x.rearrange("(t p) d -> p t d", p=P)
            for c in range(N_CHUNKS):
                g, k = divmod(c, KC)
                name, first, cols, _ = GROUPS[g]
                s = c % N_RAW
                if c < KC:
                    sp.dma_start(xT_raw[:, c, :], xT[P * c:P * c + P, :]).then_inc(xT_in[c], 16)
                if c >= N_RAW:
                    sp.wait_ge(lo_ready, c - N_RAW + 1)
                if name == "mem":
                    sp.dma_start(w_raw[:, s, 0:256], w_mk[P * k:P * k + P, :]).then_inc(raw_in[s], 16)
                    sp.dma_start(w_raw[:, s, 256:512], w_mv[P * k:P * k + P, :]).then_inc(raw_in[s], 16)
                elif name == "kwz":
                    sp.dma_start(w_raw[:, s, 0:cols - ROPE], w_in[P * k:P * k + P, first:first + cols - ROPE])\
                        .then_inc(raw_in[s], 16)
                    sp.dma_start(w_raw[:, s, cols - ROPE:cols], w_in[P * k:P * k + P, K_ROPE:K_ROPE + ROPE])\
                        .then_inc(raw_in[s], 16)
                elif name.startswith("out"):
                    row = P * OUT_ORDER[k]
                    sp.dma_start(w_raw[:, s, 0:cols], w_out[row:row + P, first:first + cols]).then_inc(raw_in[s], 16)
                else:
                    sp.dma_start(w_raw[:, s, 0:cols], w_in[P * k:P * k + P, first:first + cols])\
                        .then_inc(raw_in[s], 16)
                if c == LOADS["tab"]:
                    sp.dma_start(tab[:, :], tables).then_inc(tab_in, 16)
                if c == LOADS["x_first"]:
                    sp.dma_start(x_nat[:, 0:2, :], xv[:, 0:2, :]).then_inc(x_in, 16)
                if c == LOADS["x_rest"]:
                    sp.dma_start(x_nat[:, 2:NT, :], xv[:, 2:NT, :]).then_inc(x_in, 16)
                if c == N_IN_CHUNKS + N_RAW:
                    wait_filled(sp, ("acc", NAMES[N_IN_CHUNKS // KC - 1], NT - 1))
                    sp.dma_start(x_res[:, :, :], xv).then_inc(x_in, 16)
                if c == LOADS["mask"]:
                    wait_filled(sp, ("rel", 3 * IH - 1))
                    sp.wait_ge(mT_lo_ready, 4)
                    rows = slice(BD, BD + NT)
                    sp.dma_start(qbT[rows, :, :].rearrange("p h n -> p (h n)"), chunk_mask[0]).then_inc(mask_in, 16)
                    sp.dma_start(kbT[rows, :, :].rearrange("p h n -> p (h n)"), chunk_mask[1]).then_inc(mask_in, 16)
                if c == LOADS["mem"]:
                    sp.dma_start(mem_nat[:, :, :], mem.rearrange("(t p) d -> p t d", p=P)).then_inc(mem_in, 16)
                if c == LOADS["memT"]:
                    sp.dma_start(memT_raw[:, :, :], memT.rearrange("(k p) n -> p k n", p=P)).then_inc(memT_in, 16)
                if c == LOADS["u"]:
                    sp.dma_start(uq[:, :, :], w_uq.rearrange("(k p) n -> p k n", p=P)).then_inc(uw_in, 16)
                    sp.dma_start(ukv[:, :], w_ukv).then_inc(uw_in, 16)
            ov = out.rearrange("(t p) d -> p t d", p=P)
            for n in range(2 * NT):
                side, t = divmod(n, NT)
                wait_copied(sp, ("acc", f"out{side}", t))
                sp.dma_start(ov[:, t, 512 * side:512 * side + 512],
                             x_res[:, t, 512 * side:512 * side + 512]).then_inc(stored, 16)
            sp.wait_ge(stored, 16 * 2 * NT)

        def raw_loads(c):
            return 16 * sum(2 if NAMES[e // KC] in ("mem", "kwz") else 1 for e in range(c % N_RAW, c + 1, N_RAW))

        @block.gpsimd
        def _(pool):
            own = [0]

            def then(ins):
                own[0] += 1
                ins.then_inc(pool_own, 1)
                pool.wait_ge(pool_own, own[0])

            nc.gpsimd.memset(minus_one[:, :], -1.0)
            then(nc.gpsimd.memset(half[:, :], -0.5))

            def mean(dst, src, n):
                then(nc.gpsimd.tensor_scalar(dst, src, 1.0 / n, EPS, ALU.mult, ALU.add))

            def power(dst, src):
                return nc.gpsimd.tensor_tensor(dst, src, half[:, 0:src.shape[-1]], ALU.pow)

            def root_of(key):
                if roots.index(key):
                    pool.wait_ge(root_ready, roots.index(key))
                if key[0] == "b_q":
                    pass
                elif key in sums:
                    pool.wait_ge(sums_ready, sums.index(key) + 1)
                else:
                    wait_copied(pool, key)
                if key[0] == "x_norm":
                    x = slice(0, NT)
                    mean(msx[:, x], ssx[:, x], DM)
                    then(power(rx[:, x], msx[:, x]))
                    nc.gpsimd.tensor_tensor(rx2[:, :], rx[:, x], rx[:, x], ALU.mult)
                    nc.gpsimd.tensor_tensor(irx[:, :], msx[:, x], rx[:, x], ALU.mult).then_inc(root_ready, 1)
                if key[0] == "mem_norm":
                    m = slice(NT, NT + 2)
                    mean(msx[:, m], ssx[:, m], DM)
                    power(rx[:, m], msx[:, m]).then_inc(root_ready, 1)
                if key[0] == "c_sum":
                    mean(cr[:, :, 0], css[:, :, 0], QL)
                    mean(cr[:, :, 1], css[:, :, 1], KVL)
                    both = cr[:, :, :].rearrange("p t a -> p (t a)")
                    then(power(both, both))
                    then(nc.gpsimd.tensor_tensor(cr[:, :, :], cr[:, :, :],
                                                 rx[:, 0:NT].unsqueeze(2).broadcast_to([P, NT, 2]), ALU.mult))
                    nc.gpsimd.tensor_tensor(cr2[:, :, :], cr[:, :, :], cr[:, :, :], ALU.mult).then_inc(root_ready, 1)
                if key[0] == "b_proj":
                    t = key[1]
                    k, root = bss[:, t, BH:], br[:, t, BH:2 * BH]
                    pool.wait_ge(krot_ready, 1)
                    then(nc.gpsimd.tensor_scalar(k, k, cr2[:, t, 1:2], krss[:, t:t + 1], ALU.mult, ALU.add))
                    mean(root, k, BD)
                    then(power(root, root))
                    nc.gpsimd.tensor_scalar(br[:, t, 2 * BH:], root, cr[:, t, 1:2], None, ALU.mult)\
                        .then_inc(root_ready, 1)
                if key[0] == "b_q":
                    t = key[1]
                    q, root = bss[:, t, 0:BH], br[:, t, 0:BH]
                    then(nc.gpsimd.tensor_scalar(q, q, cr2[:, t, 0:1], None, ALU.mult))
                    mean(root, q, BD)
                    then(power(root, root))
                    nc.gpsimd.tensor_scalar(root, root, cr[:, t, 0:1], B_SCALE, ALU.mult, ALU.mult)\
                        .then_inc(root_ready, 1)
                if key[0] == "km_norm":
                    root = kr[:, NT * AH:]
                    mean(root, kss[:, NT * AH:], HD)
                    power(root, root).then_inc(root_ready, 1)
                    wait_root(pool, key)
                    k = kvm[:, :, 0:MH * HD].rearrange("p m (h d) -> p m h d", h=MH)
                    for m in range(2):
                        ins = nc.gpsimd.tensor_tensor(
                            k[:, m, :, :], k[:, m, :, :],
                            root[:, MH * m:MH * m + MH].unsqueeze(2).broadcast_to([P, MH, HD]), ALU.mult)
                    ins.then_inc(km_ready, 1)
                if key[0] == "ka_norm":
                    root = kr[:, 0:NT * AH]
                    mean(root, kss[:, 0:NT * AH], HD)
                    power(root, root).then_inc(root_ready, 1)
                    wait_root(pool, key)
                    k = ka_nat[:, :, :].rearrange("p t (h d) -> p (t h) d", h=AH)
                    nc.gpsimd.tensor_tensor(k, k, root.unsqueeze(2).broadcast_to([P, NT * AH, HD]), ALU.mult)\
                        .then_inc(ka_ready, 1)
                if key[0] in ("qa_sum", "qm_sum"):
                    n, heads, scale = (slice(0, NT * AH), AH, A_SCALE) if key[0] == "qa_sum" else \
                        (slice(NT * AH, NT * AH + NT * MH), MH, M_SCALE)
                    ms, root = qms[:, n], qr[:, n]
                    mean(ms, ms, HD)
                    then(power(root, ms))
                    if key[0] == "qa_sum":
                        pool.wait_ge(tab_in, 16)
                        then(nc.gpsimd.tensor_tensor(slope_r[:, :], ms, root, ALU.mult))
                        by_tile = slope_r[:, :].rearrange("p (t h) -> p t h", t=NT)
                        then(nc.gpsimd.tensor_tensor(by_tile, by_tile,
                                                     irx[:, :].unsqueeze(2).broadcast_to([P, NT, AH]), ALU.mult))
                        then(nc.gpsimd.tensor_tensor(slope_r[:, :], slope_r[:, :], slopes, ALU.mult))
                    by_tile = root.rearrange("p (t h) -> p t h", t=NT)
                    then(nc.gpsimd.tensor_tensor(by_tile, by_tile,
                                                 rx[:, 0:NT].unsqueeze(2).broadcast_to([P, NT, heads]), ALU.mult))
                    nc.gpsimd.tensor_scalar(root, root, scale, None, ALU.mult).then_inc(root_ready, 1)

            def bias_of(u):
                _, i, heads, keys = units[u]
                n = a_units.index(u)
                if n >= 2:
                    pool.wait_ge(max_ready, u - 1)
                if u in first_unit:
                    pool.wait_ge(dist_ready, selections.index(i) + 1)
                for m, h in enumerate(heads):
                    at_head = n % 2 * 512 + keys * m
                    ins = nc.gpsimd.tensor_tensor(
                        bias_ring[:, at_head:at_head + keys], score[:, score_at(i):score_at(i) + keys],
                        slope_r[:, i * AH + h:i * AH + h + 1].broadcast_to([P, keys]), ALU.mult)
                ins.then_inc(bias_ready, 1)

            def squares_of(event):
                if event == ("evac", "mem"):
                    wait_copied(pool, ("acc", "mem", 1))
                    square(kvm_sq[:, :, :], kvm[:, :, 0:MH * HD])
                if event == ("evac", "ka"):
                    for t in range(NT):
                        wait_copied(pool, ("acc", "ka", t))
                        square(ka_sq[:, t, :], ka_nat[:, t, :])
                if event in (("evac", "qa"), ("evac", "qm")):
                    name = event[1]
                    for j in range(banks_of(name)):
                        wait_copied(pool, ("acc", name, j))
                        q = (qaT if name == "qa" else qmT)[:, j, :]
                        square(qsT[:, j, :], q)

            def square(dst, src):
                nc.gpsimd.tensor_tensor(dst, src, src, ALU.mult).then_inc(pool_squares, 1)

            def scale_gate(u):
                branch, i = last_unit[u]
                first, n = y_cols[branch]
                heads = 2 * n
                cols = slice(stat(branch, i, 0), stat(branch, i, 0) + heads)
                if branch == "A":
                    pool.wait_ge(exp_ready, a_units.index(u) + 1)
                else:
                    wait_copied(pool, ("S", u))
                wait_copied(pool, ("acc", {"A": "kwz", "B": "zb", "M": "zm"}[branch], i))
                then(nc.gpsimd.tensor_tensor(rowinv[:, cols], rowsum[:, cols], minus_one[:, 0:heads], ALU.pow))
                y = gates[:, i, P * first:P * (first + n)].rearrange("p (h d) -> p h d", h=heads)
                nc.gpsimd.tensor_tensor(y, y, rowinv[:, cols].unsqueeze(2).broadcast_to([P, heads, HD]), ALU.mult)\
                    .then_inc(gate_scaled, 1)

            for c in range(N_CHUNKS):
                for event in at[c]:
                    squares_of(event)
                    if event[0] == "step" and event[1] - SCALE_GATE in last_unit:
                        scale_gate(event[1] - SCALE_GATE)
                    if event in roots:
                        root_of(event)
                    if event[0] == "b_proj":
                        root_of(("b_q",) + event[1:])
                    if event[0] == "step" and event[1] + 2 in a_units:
                        bias_of(event[1] + 2)

        @block.scalar
        def _(act):
            act.dma_start(gain[:, 0:GAIN_COLS], gains[:, 0:GAIN_COLS]).then_inc(gain_in, 16)
            act.dma_start(gain[:, GAIN_COLS:], gains[:, GAIN_COLS:]).then_inc(rows_in, 16)
            own = [0]

            def mark(ins):
                own[0] += 1
                ins.then_inc(act_own, 1)
                return own[0]

            def split_hi(c):
                cols = GROUPS[c // KC][2]
                act.wait_ge(raw_in[c % N_RAW], raw_loads(c))
                if c >= N_SPLIT:
                    wait_chunk_used(act, c - N_SPLIT)
                factor = 1.0 if gain_of(c) is None else gain_of(c)
                nc.scalar.activation(w_hi[:, c % N_SPLIT, 0:cols], w_raw[:, c % N_RAW, 0:cols],
                                     ACT.Copy, scale=factor).then_inc(hi_ready, 1)

            def x_hi(k):
                act.wait_ge(xT_in[k], 16)
                nc.scalar.activation(hT_hi[:, k, :], xT_raw[:, k, :], ACT.Copy).then_inc(xT_hi_ready, 1)

            def copy_out(key, dst, src, func=ACT.Copy, **kw):
                nc.scalar.activation(dst, src, func, **kw).then_inc(free(key), 1)

            act.wait_ge(pool_own, 1)
            nc.scalar.activation(table_load[:, :], half[:, 0:1], ACT.Copy)

            def scalar_event(event):
                kind = event[0]
                if kind == "x_norm":
                    act.wait_ge(x_in, 32)
                    for t in range(NT):
                        ins = nc.scalar.activation(squares[:, :], x_nat[:, t, :], ACT.Square, accum_out=ssx[:, t:t + 1])
                        if t < NT - 1:
                            act.wait_ge(act_own, mark(ins))
                    ins.then_inc(sums_ready, 1)
                if kind == "u_split":
                    act.wait_ge(uw_in, 32)
                    act.wait_ge(sums_ready, 1)
                    nc.scalar.activation(uq_hi[:, :, :], uq[:, :, :], ACT.Copy).then_inc(u_hi_ready, 1)
                    nc.scalar.activation(ukv_hi[:, :], ukv[:, :], ACT.Copy).then_inc(u_hi_ready, 1)
                if kind == "mem_norm":
                    act.wait_ge(mem_in, 16)
                    act.wait_ge(sums_ready, 1)
                    act.wait_ge(act_own, mark(nc.scalar.activation(
                        squares[:, :], mem_nat[:, 0, :], ACT.Square, accum_out=ssx[:, NT:NT + 1])))
                    nc.scalar.activation(squares[:, :], mem_nat[:, 1, :], ACT.Square,
                                         accum_out=ssx[:, NT + 1:NT + 2]).then_inc(sums_ready, 1)
                if kind == "mem_split":
                    act.wait_ge(memT_in, 16)
                    for n in range(4):
                        nc.scalar.activation(mT_hi[:, 2 * n:2 * n + 2, :], memT_raw[:, 2 * n:2 * n + 2, :], ACT.Copy)\
                            .then_inc(mT_hi_ready, 1)
                if kind == "evac" and not event[1].startswith("out"):
                    name = event[1]
                    if name == "kwz":
                        wait_root(act, ("x_norm",))
                    if name == "mem":
                        wait_root(act, ("mem_norm",))
                    if name == "c":
                        act.wait_ge(sums_ready, 2)
                    if name == "kwz":
                        for j in range(NT):
                            bank = wait_filled(act, ("acc", name, j))
                            nc.scalar.activation(kidx_nat[:, j, :].rearrange("p (a d) -> p a d", a=2),
                                                 bank[:, 0:HD].unsqueeze(1).broadcast_to([P, 2, HD]), ACT.Copy,
                                                 scale=rx[:, j:j + 1]).then_inc(kidx_ready, 1)
                    for j in range(banks_of(name)):
                        key = ("acc", name, j)
                        bank = wait_filled(act, key)
                        r = rx[:, j:j + 1]
                        if name == "idx":
                            for part in (slice(0, HD), slice(HD, P)):
                                h = 2 * j + part.start // HD
                                nc.scalar.activation(qidx_parts[part, h, :], bank[part, :], ACT.Copy)\
                                    .then_inc(idx_hi_ready, 1)
                        if name == "kwz":
                            nc.scalar.activation(w_idx[:, j, :], bank[:, HD:HD + IH], ACT.Copy, scale=rx2[:, j:j + 1])
                            nc.scalar.activation(krope[:, j, :], bank[:, 456:488], ACT.Copy, scale=r)
                            copy_out(key, gates[:, j, 0:384], bank[:, HD + IH:456], ACT.Silu, scale=r)
                        if name == "c":
                            nc.scalar.activation(qsT[:, j, :], bank[:, :], ACT.Square)
                            nc.scalar.activation(cT_hi[:, j, :], bank[:, :], ACT.Copy,
                                                 scale=gain[:, G_CQ + j:G_CQ + j + 1]).then_inc(c_hi_ready, 1)
                        if name == "mem":
                            copy_out(key, kvm[:, j, :], bank[:, :], scale=rx[:, NT + j:NT + j + 1])
                        if name == "zb":
                            copy_out(key, gates[:, j, 384:768], bank[:, 0:384], ACT.Silu, scale=r)
                        if name == "ka":
                            copy_out(key, ka_nat[:, j, :], bank[:, 0:384], scale=r)
                        if name == "qa":
                            copy_out(key, qaT[:, j, :], bank[:, :])
                        if name == "va":
                            copy_out(key, va[:, j, :], bank[:, 0:384], scale=r)
                        if name == "qm":
                            copy_out(key, qmT[:, j, :], bank[:, :])
                        if name == "zm":
                            copy_out(key, gates[:, j, 768:1024], bank[:, 0:256], ACT.Silu, scale=r)
                if kind == "kidx_T":
                    nc.scalar.activation(kidx_hi[:, :], wait_filled(act, event)[:, :], ACT.Copy)\
                        .then_inc(idx_hi_ready, 1)
                if kind == "rel":
                    u = event[1]
                    keys = P * (2 + u // IH)
                    bank = wait_filled(act, event)
                    if u >= N_RELU:
                        act.wait_ge(relu_used, u - N_RELU + 1)
                    copy_out(event, relu_ring[:, u % N_RELU, 0:keys], bank[:, 0:keys], ACT.Relu)
                if kind == "b_proj":
                    t = event[1]
                    if t:
                        act.wait_ge(b_nat_ready, t)
                    for j in range(2):
                        bank = wait_filled(act, (kind, t, j))
                        nc.scalar.activation(head_sq[:, 288 * j:288 * j + 288], bank[:, 0:288], ACT.Square)
                    for j in range(2):
                        bank = wait_filled(act, (kind, t, 2 + j))[:, 0:384].rearrange("p (h c) -> p h c", h=3)
                        ins = nc.scalar.activation(
                            head_sq[:, 576 + 192 * j:768 + 192 * j].rearrange("p (h d) -> p h d", h=3),
                            bank[:, :, 0:HD], ACT.Square)
                    ins.then_inc(squares_ready, 1)
                    wait_root(act, ("c_sum",))
                    for j in range(2):
                        bank = psum[6 + j][:, 0:384].rearrange("p (h c) -> p h c", h=3)
                        ins = nc.scalar.activation(vb[:, t, 192 * j:192 * j + 192].rearrange("p (h d) -> p h d", h=3),
                                                   bank[:, :, HD:2 * HD], ACT.Copy, scale=cr[:, t, 1:2])
                    ins.then_inc(b_scalar_done, 1)
                if kind == "b_T":
                    t = event[1]
                    for j in range(3):
                        key = (kind, t, j)
                        bank = wait_filled(act, key)[0:BD, :].rearrange("p (h n) -> p h n", h=4)
                        if j == 0:
                            copy_out(key, qbT[0:BD, 0:4, tile(t)], bank)
                        if j == 1:
                            nc.scalar.activation(qbT[0:BD, 4:6, tile(t)], bank[:, 0:2, :], ACT.Copy)
                            copy_out(key, kbT[0:BD, 0:2, tile(t)], bank[:, 2:4, :])
                        if j == 2:
                            copy_out(key, kbT[0:BD, 2:6, tile(t)], bank)
                if kind == "km_T":
                    copy_out(event, kmT[:, :, :].rearrange("p j n -> p (j n)"), wait_filled(act, event)[:, :],
                             scale=kgain[:, 1:2])
                if kind == "ka_T":
                    copy_out(event, kaT[:, event[1], :], wait_filled(act, event)[:, :], scale=kgain[:, 0:1])
                if kind == "step":
                    s = event[1]
                    if s - TURN_Y in last_unit:
                        branch, i = last_unit[s - TURN_Y]
                        first, n = y_cols[branch]
                        bank = wait_filled(act, ("y_T", branch, i))
                        nc.scalar.activation(yT[branch][0][:, :, tile(i)],
                                             bank[:, 0:P * n].rearrange("p (k n) -> p k n", k=n), ACT.Copy)\
                            .then_inc(yT_hi_ready, 1)
                    if 0 <= s - TRANSPOSE < N_UNITS:
                        u = s - TRANSPOSE
                        n = units[u][3] * len(units[u][2])
                        bank = wait_filled(act, ("PT", u))
                        if u >= 3:
                            act.wait_ge(pv_done, u - 2)
                        copy_out(("PT", u), probT[:, u % 3, 0:n], bank[:, 0:n])
                    if s < N_UNITS:
                        exponent(s)

            def exponent(u):
                branch, i, heads, keys = units[u]
                act.wait_ge(max_ready, u + 1)
                if u >= 3:
                    wait_filled(act, ("PT", u - 3))
                bank = psum[uses["S", u][0]]
                for n, head in enumerate(heads):
                    col = stat(branch, i, head)
                    cols = slice(keys * n, keys * n + keys)
                    src = prob[:, u % 3, cols] if branch == "A" else bank[:, cols]
                    ins = nc.scalar.activation(prob[:, u % 3, cols], src, ACT.Exp, bias=negmax[:, col:col + 1],
                                               scale=score_scale(branch, i, [head]), accum_out=rowsum[:, col:col + 1])
                ins.then_inc(exp_ready if branch == "A" else free(("S", u)), 1)

            for c in range(N_CHUNKS + LEAD_HI):
                if c < KC:
                    x_hi(c)
                if c == 0:
                    act.wait_ge(gain_in, 16)
                if c < N_CHUNKS:
                    split_hi(c)
                if c == LEAD_HI:
                    act.wait_ge(consts_ready, 1)
                for event in at.get(c - LEAD_HI, []):
                    scalar_event(event)

        @block.vector
        def _(dve):
            own = [0]

            def mark(ins):
                own[0] += 1
                ins.then_inc(dve_own, 1)
                return own[0]

            def then(ins):
                dve.wait_ge(dve_own, mark(ins))

            def low_part(dst, src, hi):
                return nc.vector.tensor_tensor(dst, src, hi.bitcast(F32), ALU.subtract)

            def split_lo(c):
                cols = GROUPS[c // KC][2]
                dve.wait_ge(hi_ready, c + 1)
                dst, src = w_lo[:, c % N_SPLIT, 0:cols], w_raw[:, c % N_RAW, 0:cols]
                hi = w_hi[:, c % N_SPLIT, 0:cols]
                if gain_of(c) is None:
                    low_part(dst, src, hi).then_inc(lo_ready, 1)
                else:
                    nc.vector.scalar_tensor_tensor(dst, src, gain_of(c), hi.bitcast(F32), ALU.mult, ALU.subtract)\
                        .then_inc(lo_ready, 1)

            def x_lo(k):
                dve.wait_ge(xT_hi_ready, k + 1)
                low_part(hT_lo[:, k, :], xT_raw[:, k, :], hT_hi[:, k, :]).then_inc(xT_lo_ready, 1)

            q_row, k_row = gain[:, GAIN_COLS:GAIN_COLS + BD], gain[:, GAIN_COLS + BD:GAIN_COLS + 2 * BD]

            def make_constants():
                dve.wait_ge(gain_in, 16)
                dve.wait_ge(rows_in, 16)
                nc.vector.tensor_tensor(kgain[:, 0:1], gain[:, G_QA:G_QA + 1], gain[:, G_KA:G_KA + 1], ALU.mult)
                nc.vector.tensor_tensor(kgain[:, 1:2], gain[:, G_QM:G_QM + 1], gain[:, G_KM:G_KM + 1], ALU.mult)
                nc.vector.tensor_tensor(qb_row[:, 0:HD], q_row[:, 0:HD], k_row[:, 0:HD], ALU.mult)
                nc.vector.tensor_copy(qb_row[:, HD:BD], q_row[:, HD:BD]).then_inc(consts_ready, 1)
                dve.wait_ge(consts_ready, 1)

            topk_mark = [0] * 3

            def rotate(part, tmp, cos, sin, whole):
                n = ROPE // 2
                nc.vector.tensor_tensor(tmp[0], part, cos, ALU.mult)
                nc.vector.tensor_tensor(tmp[1][:, :, 0:n], part[:, :, n:ROPE], sin[:, :, 0:n], ALU.mult)
                then(nc.vector.tensor_tensor(tmp[1][:, :, n:ROPE], part[:, :, 0:n], sin[:, :, n:ROPE], ALU.mult))
                return nc.vector.tensor_tensor(whole, tmp[0], tmp[1], ALU.add)

            def vector_event(event):
                kind = event[0]
                if kind == "mem_split":
                    for n in range(4):
                        dve.wait_ge(mT_hi_ready, n + 1)
                        ks = slice(2 * n, 2 * n + 2)
                        low_part(mT_lo[:, ks, :], memT_raw[:, ks, :], mT_hi[:, ks, :]).then_inc(mT_lo_ready, 1)
                if kind == "u_split":
                    dve.wait_ge(u_hi_ready, 1)
                    low_part(uq_lo[:, :, :], uq[:, :, :], uq_hi[:, :, :]).then_inc(u_lo_ready, 1)
                    dve.wait_ge(u_hi_ready, 2)
                    low_part(ukv_lo[:, :], ukv[:, :], ukv_hi[:, :]).then_inc(u_lo_ready, 1)
                if event == ("evac", "c"):
                    for j in range(3):
                        key = ("acc", "c", j)
                        bank = wait_filled(dve, key)
                        dve.wait_ge(c_hi_ready, j + 1)
                        nc.vector.scalar_tensor_tensor(cT_lo[:, j, :], bank[:, :], gain[:, G_CQ + j:G_CQ + j + 1],
                                                       cT_hi[:, j, :].bitcast(F32), ALU.mult, ALU.subtract)\
                            .then_inc(free(key), 1)
                if event == ("evac", "idx"):
                    for h in range(IH):
                        key = ("acc", "idx", h // 2)
                        part = slice(HD * (h % 2), HD * (h % 2) + HD)
                        other = slice(HD - part.start, P - part.start)
                        bank = wait_filled(dve, key)
                        dve.wait_ge(idx_hi_ready, 2 * (h // 2) + 2)
                        ins = low_part(qidx_parts[other, h, :], bank[part, :], qidx_parts[part, h, :])
                        if h % 2:
                            ins.then_inc(free(key), 1)
                if kind == "kidx_T":
                    bank = wait_filled(dve, event)
                    dve.wait_ge(idx_hi_ready, IH + 1)
                    low_part(kidx_lo[:, :], bank[:, :], kidx_hi[:, :]).then_inc(free(event), 1)
                if kind == "evac" and event[1].startswith("out"):
                    side = int(event[1][3:])
                    dve.wait_ge(x_in, 48)
                    for t in range(NT):
                        key = ("acc", event[1], t)
                        dst = x_res[:, t, 512 * side:512 * side + 512]
                        nc.vector.tensor_tensor(dst, wait_filled(dve, key)[:, :], dst, ALU.add).then_inc(free(key), 1)
                if kind == "rel":
                    u = event[1]
                    i, h = 1 + u // IH, u % IH
                    keys = P * (i + 1)
                    s = score[:, score_at(i):score_at(i) + keys]
                    wait_copied(dve, event)
                    if h == 0:
                        nc.vector.tensor_scalar(s, relu_ring[:, u % N_RELU, 0:keys], w_idx[:, i, 0:1], None, ALU.mult)\
                            .then_inc(relu_used, 1)
                    else:
                        dve.wait_ge(relu_used, u)
                        nc.vector.scalar_tensor_tensor(s, relu_ring[:, u % N_RELU, 0:keys], w_idx[:, i, h:h + 1], s,
                                                       ALU.mult, ALU.add).then_inc(relu_used, 1)
                    if h == IH - 1:
                        dve.wait_ge(relu_used, u + 1)
                        topk_mark[i - 1] = mark(nc.vector.memset(s[0:64, keys - 64:keys], INADMISSIBLE))
                if kind == "topk":
                    b = event[1] - 1
                    s = score[:, score_at(b + 1):score_at(b + 2)]
                    dve.wait_ge(dve_own, topk_mark[b])
                    then(nc.vector.max(top8[:, b, :], s))
                    topk_mark[b] = mark(nc.vector.match_replace(s, top8[:, b, :], s, MARK))
                if kind == "krope":
                    dve.wait_ge(tab_in, 16)
                    wait_copied(dve, ("acc", "kwz", NT - 1))
                    then(nc.vector.tensor_tensor(krot_tmp[:, 0, :, :], krope[:, :, :], krope[:, :, :], ALU.mult))
                    nc.vector.tensor_reduce(krss[:, :], krot_tmp[:, 0, :, :], AX.X, ALU.add)
                    row = k_row[:, HD:BD].unsqueeze(1).broadcast_to([P, NT, ROPE])
                    then(nc.vector.tensor_tensor(krot[:, :, :], krope[:, :, :], row, ALU.mult))
                    rotate(krot[:, :, :], (krot_tmp[:, 0, :, :], krot_tmp[:, 1, :, :]),
                           rope_tab[:, :, 0:ROPE], rope_tab[:, :, ROPE:], krot[:, :, :]).then_inc(krot_ready, 1)
                if kind == "b_proj":
                    t = event[1]
                    dve.wait_ge(squares_ready, t + 1)
                    nc.vector.tensor_reduce(bss[:, t, 0:BH], head_sq[:, 0:576].rearrange("p (h d) -> p h d", h=BH),
                                            AX.X, ALU.add)
                    nc.vector.tensor_reduce(bss[:, t, BH:], head_sq[:, 576:960].rearrange("p (h d) -> p h d", h=BH),
                                            AX.X, ALU.add).then_inc(sums_ready, 1)
                    dve.wait_ge(sums_ready, sums.index(event) + 1)
                    dve.wait_ge(b_scalar_done, t + 1)
                    if t:
                        wait_filled(dve, ("b_T", t - 1, 2))
                    for j in range(2):
                        key = (kind, t, j)
                        nc.vector.tensor_tensor(
                            q_nat[:, 3 * j:3 * j + 3, :], wait_filled(dve, key)[:, 0:288].rearrange("p (h d) -> p h d", h=3),
                            qb_row[:, :].unsqueeze(1).broadcast_to([P, 3, BD]), ALU.mult).then_inc(free(key), 1)
                    wait_copied(dve, (kind, t, 1))
                    cos = rope_tab[:, t, 0:ROPE].unsqueeze(1).broadcast_to([P, BH, ROPE])
                    sin = rope_tab[:, t, ROPE:].unsqueeze(1).broadcast_to([P, BH, ROPE])
                    rotate(q_nat[:, :, HD:BD], (rope_tmp[:, 0, :, :], rope_tmp[:, 1, :, :]), cos, sin,
                           q_nat[:, :, HD:BD])
                if kind == "b_scale":
                    t = event[1]
                    wait_root(dve, ("b_proj", t))
                    for j in range(2):
                        key = ("b_proj", t, 2 + j)
                        r = br[:, t, 2 * BH + 3 * j:2 * BH + 3 * j + 3].unsqueeze(2).broadcast_to([P, 3, HD])
                        nc.vector.tensor_tensor(
                            k_nat[:, 3 * j:3 * j + 3, 0:HD],
                            wait_filled(dve, key)[:, 0:384].rearrange("p (h c) -> p h c", h=3)[:, :, 0:HD],
                            r, ALU.mult).then_inc(free(key), 1)
                    dve.wait_ge(krot_ready, 1)
                    nc.vector.tensor_tensor(k_nat[:, :, HD:BD], krot[:, t, :].unsqueeze(1).broadcast_to([P, BH, ROPE]),
                                            br[:, t, BH:2 * BH].unsqueeze(2).broadcast_to([P, BH, ROPE]), ALU.mult)\
                        .then_inc(b_nat_ready, 1)
                if kind == "km_norm":
                    dve.wait_ge(pool_squares, squared.index(("km",)) + 1)
                    nc.vector.tensor_reduce(kss[:, NT * AH:], kvm_sq[:, :, :].rearrange("p m (h d) -> p (m h) d", h=MH),
                                            AX.X, ALU.add).then_inc(sums_ready, 1)
                if kind == "ka_norm":
                    for t in (2, 3):
                        ins = ka_sums(t)
                    ins.then_inc(sums_ready, 1)
                if kind == "ka_sums":
                    for t in (0, 1):
                        ka_sums(t)
                if kind == "c_sum":
                    wait_root(dve, ("x_norm",))
                    nc.vector.tensor_tensor(css[:, :, :],
                                            wait_filled(dve, event)[:, 0:2 * NT].rearrange("p (t a) -> p t a", t=NT),
                                            rx2[:, :].unsqueeze(2).broadcast_to([P, NT, 2]), ALU.mult)\
                        .then_inc(free(event), 1)
                if kind[:3] in ("qa_", "qm_"):
                    lo, heads = (0, AH) if kind.startswith("qa") else (NT * AH, MH)
                    ts = slice(0, 2) if kind.endswith("first") else slice(2, 4)
                    n = 2 * heads
                    lo += ts.start * heads
                    nc.vector.tensor_tensor(qms[:, lo:lo + n].rearrange("p (t h) -> p t h", t=2),
                                            wait_filled(dve, event)[:, 0:n].rearrange("p (t h) -> p t h", t=2),
                                            rx2[:, ts].unsqueeze(2).broadcast_to([P, 2, heads]), ALU.mult)\
                        .then_inc(free(event), 1)
                if kind == "distances":
                    i = event[1]
                    s = score[:, score_at(i):score_at(i + 1)]
                    if i == 0:
                        dve.wait_ge(tab_in, 16)
                        then(nc.vector.tensor_copy(s, ndist[:, 512 - P:512]))
                        nc.vector.memset(s[0:64, P - 64:P], NEG).then_inc(dist_ready, 1)
                    else:
                        dve.wait_ge(dve_own, topk_mark[i - 1])
                        then(nc.vector.tensor_scalar(s, s, MARKED_BELOW, NEG, ALU.is_gt, ALU.mult))
                        nc.vector.tensor_tensor(s, s, ndist[:, 512 - P * (i + 1):512], ALU.add).then_inc(dist_ready, 1)
                if kind == "step":
                    s = event[1]
                    if s - TURN_Y in last_unit:
                        branch, i = last_unit[s - TURN_Y]
                        first, n = y_cols[branch]
                        key = ("y_T", branch, i)
                        bank = wait_filled(dve, key)
                        dve.wait_ge(yT_hi_ready, y_number[branch, i] + 1)
                        hi, lo = yT[branch]
                        low_part(lo[:, :, tile(i)], bank[:, 0:P * n].rearrange("p (k n) -> p k n", k=n),
                                 hi[:, :, tile(i)]).then_inc(free(key), 1)
                    if s < N_UNITS:
                        row_max(s)
                    if s - SCALE_Y in last_unit:
                        scale_y(s - SCALE_Y)

            def ka_sums(t):
                dve.wait_ge(pool_squares, squared.index(("ka", t)) + 1)
                return nc.vector.tensor_reduce(kss[:, AH * t:AH * t + AH],
                                               ka_sq[:, t, :].rearrange("p (h d) -> p h d", h=AH), AX.X, ALU.add)

            def row_max(u):
                branch, i, heads, keys = units[u]
                bank = wait_filled(dve, ("S", u))
                if u in first_unit:
                    wait_root(dve, {"B": ("b_q", i), "M": ("qm_sum",), "A": ("qa_sum",)}[branch])
                cols = stats_of(branch, i, heads)
                if branch == "A":
                    n = a_units.index(u)
                    dve.wait_ge(bias_ready, n + 1)
                    wait_filled(dve, ("PT", u - 3))
                    for m, h in enumerate(heads):
                        col = stat(branch, i, h)
                        part = slice(keys * m, keys * m + keys)
                        at_head = n % 2 * 512 + keys * m
                        ins = nc.vector.tensor_tensor_reduce(
                            out=prob[:, u % 3, part], in0=bank[:, part], in1=bias_ring[:, at_head:at_head + keys],
                            scale=1.0, scalar=-3.4e38, op0=ALU.add, op1=ALU.max, accum_out=rowmax[:, col:col + 1])
                    ins.then_inc(free(("S", u)), 1)
                    wait_copied(dve, ("S", u))
                else:
                    by_head = bank[:, 0:keys * len(heads)].rearrange("p (h n) -> p h n", h=len(heads))
                    then(nc.vector.tensor_reduce(rowmax[:, cols], by_head, AX.X, ALU.max))
                nc.vector.scalar_tensor_tensor(negmax[:, cols], rowmax[:, cols], -1.0, score_scale(branch, i, heads),
                                               ALU.mult, ALU.mult).then_inc(max_ready, 1)

            def scale_y(u):
                branch, i = last_unit[u]
                first, n = y_cols[branch]
                heads = 2 * n
                dve.wait_ge(pv_done, u + 1)
                dve.wait_ge(gate_scaled, y_number[branch, i] + 1)
                y = gates[:, i, P * first:P * (first + n)].rearrange("p (h d) -> p h d", h=heads)
                bank = psum[uses["O", branch, i][0]]
                nc.vector.tensor_tensor(y, bank[:, 0:HD * heads].rearrange("p (h d) -> p h d", h=heads), y,
                                        ALU.mult).then_inc(free(("O", branch, i)), 1)

            nc.vector.memset(zeros[:, :], 0.0).then_inc(zeros_ready, 1)
            for c in range(N_CHUNKS + LEAD):
                if c < KC:
                    x_lo(c)
                if c < N_CHUNKS:
                    split_lo(c)
                if c == 4:
                    make_constants()
                for event in at.get(c - LEAD, []):
                    vector_event(event)

        @block.tensor
        def _(pe):
            def transpose(dst, src):
                return nc.tensor.transpose(dst, src, ident)

            def project(c, halfway):
                g, k = divmod(c, KC)
                name, _, cols, transposed = GROUPS[g]
                s = c % N_SPLIT
                hi_w, lo_w = w_hi[:, s, 0:cols], w_lo[:, s, 0:cols]
                hi_t, lo_t = (mT_hi, mT_lo) if name == "mem" else (hT_hi, hT_lo)
                row = k
                if name == "idx":
                    pe.wait_ge(xT_hi_ready, k + 1)
                if name == "mem":
                    pe.wait_ge(mT_lo_ready, k // 2 + 1)
                if name.startswith("out"):
                    branch, first = [(b, first) for b, (first, n) in y_cols.items()
                                     if first <= OUT_ORDER[k] < first + n][0]
                    hi_t, lo_t = yT[branch]
                    row = OUT_ORDER[k] - first
                    if name == "out0" and row == 0:
                        wait_copied(pe, ("y_T", branch, NT - 1))
                pe.wait_ge(hi_ready, c + 1)
                for j in range(banks_of(name)):
                    key = ("acc", name, j)
                    bank = psum[uses[key][0]]
                    if k == 0:
                        wait_free(pe, key)
                    if transposed:
                        dst = bank[:, :]
                        passes = [(hi_w[:, tile(j)], hi_t[:, row, :]), (hi_w[:, tile(j)], lo_t[:, row, :]),
                                  (lo_w[:, tile(j)], hi_t[:, row, :])]
                    else:
                        dst = bank[:, 0:cols]
                        passes = [(hi_t[:, row, tile(j)], hi_w), (hi_t[:, row, tile(j)], lo_w),
                                  (lo_t[:, row, tile(j)], hi_w)]
                    for n, (stationary, moving) in enumerate(passes):
                        if j == 0 and n == 1:
                            pe.wait_ge(lo_ready, c + 1)
                        ins = nc.tensor.matmul(dst, stationary, moving, start=(k == 0 and n == 0),
                                               stop=(k == KC - 1 and n == 2))
                    if k == KC - 1:
                        ins.then_inc(filled(key), 1)
                    elif j == banks_of(name) - 1:
                        ins.then_inc(chunk_used, 1)
                    if j == 1:
                        for event in halfway:
                            tensor_event(event)

            def tensor_event(event):
                kind = event[0]
                if kind == "kidx_T":
                    pe.wait_ge(tab_in, 16)
                    pe.wait_ge(kidx_ready, NT)
                    bank = wait_free(pe, event)
                    for t in range(NT):
                        ins = transpose(bank[:, tile(t)], kidx_nat[:, t, :])
                    ins.then_inc(filled(event), 1)
                if kind == "rel":
                    u = event[1]
                    i, h = 1 + u // IH, u % IH
                    keys = P * (i + 1)
                    if u == 0:
                        wait_copied(pe, ("kidx_T",))
                        wait_copied(pe, ("acc", "idx", 3))
                    bank = wait_free(pe, event)
                    q = qidx_parts[:, h, tile(i)]
                    nc.tensor.matmul(bank[:, 0:keys], q, kidx_hi[:, 0:keys], start=True, stop=False)
                    nc.tensor.matmul(bank[:, 0:keys], q, kidx_lo[:, 0:keys], start=False, stop=True)\
                        .then_inc(filled(event), 1)
                if kind == "c_sum":
                    wait_copied(pe, ("acc", "c", 2))
                    bank = wait_free(pe, event)
                    for t in range(NT):
                        for j in range(3):
                            col = 2 * t + j // 2
                            ins = nc.tensor.matmul(bank[:, col:col + 1], qsT[:, j, tile(t)], ones1,
                                                   start=(j != 1), stop=(j != 0))
                    ins.then_inc(filled(event), 1)
                if kind == "b_proj":
                    t = event[1]
                    if t == 0:
                        pe.wait_ge(u_lo_ready, 2)
                        wait_copied(pe, ("acc", "c", 2))
                    for j in range(4):
                        key = (kind, t, j)
                        bank = wait_free(pe, key)
                        if j < 2:
                            cols = slice(288 * j, 288 * j + 288)
                            parts = [(k, uq_hi[:, k, cols], uq_lo[:, k, cols]) for k in range(2)]
                        else:
                            cols = slice(384 * (j - 2), 384 * (j - 2) + 384)
                            parts = [(2, ukv_hi[:, cols], ukv_lo[:, cols])]
                        for k, u_hi, u_lo in parts:
                            dst = bank[:, 0:cols.stop - cols.start]
                            hi, lo = cT_hi[:, k, tile(t)], cT_lo[:, k, tile(t)]
                            nc.tensor.matmul(dst, hi, u_hi, start=(k != 1), stop=False)
                            nc.tensor.matmul(dst, hi, u_lo, start=False, stop=False)
                            ins = nc.tensor.matmul(dst, lo, u_hi, start=False, stop=(k != 0))
                        ins.then_inc(filled(key), 1)
                if kind == "b_T":
                    t = event[1]
                    pe.wait_ge(b_nat_ready, t + 1)
                    for j in range(3):
                        key = (kind, t, j)
                        bank = wait_free(pe, key)
                        for n in range(4):
                            m = 4 * j + n
                            src = q_nat[:, m, :] if m < BH else k_nat[:, m - BH, :]
                            ins = transpose(bank[0:BD, tile(n)], src)
                        ins.then_inc(filled(key), 1)
                if kind == "km_T":
                    pe.wait_ge(km_ready, 1)
                    bank = wait_free(pe, event)
                    for j in range(2):
                        for m in range(2):
                            ins = transpose(bank[:, tile(2 * j + m)], kvm[:, m, P * j:P * j + P])
                    ins.then_inc(filled(event), 1)
                if kind == "ka_T":
                    pe.wait_ge(ka_ready, 1)
                    j = event[1]
                    bank = wait_free(pe, event)
                    for t in range(NT):
                        ins = transpose(bank[:, tile(t)], ka_nat[:, t, P * j:P * j + P])
                    ins.then_inc(filled(event), 1)
                if kind[:3] in ("qa_", "qm_"):
                    name, tiles = ("qa", 3) if kind.startswith("qa") else ("qm", 2)
                    pe.wait_ge(pool_squares, squared.index((name, tiles - 1)) + 1)
                    bank = wait_free(pe, event)
                    for n, t in enumerate((0, 1) if kind.endswith("first") else (2, 3)):
                        for j in range(tiles):
                            col = 2 * (tiles * n + j)
                            ins = nc.tensor.matmul(bank[:, col:col + 2], qsT[:, j, tile(t)], ones2,
                                                   start=True, stop=True)
                    ins.then_inc(filled(event), 1)

                if kind == "step":
                    s = event[1]
                    turns_y = s - TURN_Y in last_unit
                    if turns_y:
                        branch, i = last_unit[s - TURN_Y]
                        first, n = y_cols[branch]
                        wait_copied(pe, ("O", branch, i))
                        bank = wait_free(pe, ("y_T", branch, i))
                        for m in range(n):
                            ins = transpose(bank[:, tile(m)], gates[:, i, P * (first + m):P * (first + m) + P])
                        ins.then_inc(filled(("y_T", branch, i)), 1)
                    if 0 <= s - TRANSPOSE < N_UNITS and not turns_y:
                        transpose_probs(s - TRANSPOSE)
                    if s < N_UNITS:
                        scores(s)
                    if 0 <= s - WEIGH < N_UNITS:
                        weigh_values(s - WEIGH)
                    if 0 <= s - TRANSPOSE < N_UNITS and turns_y:
                        transpose_probs(s - TRANSPOSE)

            def scores(u):
                branch, i, heads, keys = units[u]
                if u in first_unit:
                    if branch == "B":
                        wait_copied(pe, ("b_T", i, 2))
                        pe.wait_ge(mask_in, 32)
                    if branch == "M" and i == 0:
                        wait_copied(pe, ("acc", "qm", 1))
                        wait_copied(pe, ("km_T",))
                    if branch == "A" and i == 0:
                        wait_copied(pe, ("acc", "qa", 2))
                        wait_copied(pe, ("ka_T", 2))
                bank = wait_free(pe, ("S", u))
                for n, head in enumerate(heads):
                    half_ = slice(HD * (head % 2), HD * (head % 2) + HD)
                    if branch == "B":
                        q, k = qbT[0:BD + NT, head, tile(i)], kbT[0:BD + NT, head, 0:keys]
                    if branch == "M":
                        q, k = qmT[half_, head // 2, tile(i)], kmT[half_, head // 2, :]
                    if branch == "A":
                        q, k = qaT[half_, head // 2, tile(i)], kaT[half_, head // 2, 0:keys]
                    ins = nc.tensor.matmul(bank[:, keys * n:keys * n + keys], q, k, start=True, stop=True)
                ins.then_inc(filled(("S", u)), 1)

            def transpose_probs(u):
                branch, _, heads, keys = units[u]
                if branch == "A":
                    pe.wait_ge(exp_ready, a_units.index(u) + 1)
                else:
                    wait_copied(pe, ("S", u))
                bank = wait_free(pe, ("PT", u))
                for n in range(keys * len(heads) // P):
                    ins = transpose(bank[:, tile(n)], prob[:, u % 3, tile(n)])
                ins.then_inc(filled(("PT", u)), 1)

            def weigh_values(u):
                branch, i, heads, keys = units[u]
                wait_copied(pe, ("PT", u))
                if branch == "A" and u in first_unit:
                    wait_copied(pe, ("acc", "va", i))
                if u in first_unit:
                    wait_free(pe, ("O", branch, i))
                bank = psum[uses["O", branch, i][0]]
                tiles = keys // P
                for n, head in enumerate(heads):
                    for m in range(tiles):
                        v = {"A": va, "B": vb, "M": kvm}[branch]
                        col = HD * head + (MH * HD if branch == "M" else 0)
                        ins = nc.tensor.matmul(bank[:, HD * head:HD * head + HD], probT[:, u % 3, tile(tiles * n + m)],
                                               v[:, m, col:col + HD], start=(m == 0), stop=(m == tiles - 1))
                ins.then_inc(pv_done, 1)

            pe.wait_ge(zeros_ready, 1)
            for n in WARM_UP:
                nc.tensor.matmul(psum[7][:, 0:n], zeros[:, 0:P], zeros[:, 0:n], start=True, stop=True)
            for c in range(N_CHUNKS):
                first_half, second_half = [], at[c]
                if c >= TWO_STEPS_FROM:
                    first_half, second_half = at[c][:1], at[c][1:]
                project(c, first_half)
                for event in second_half:
                    tensor_event(event)


def kernel(**inputs):
    import numpy as np
    import concourse.bacc as bacc
    from concourse.bass_utils import run_bass_kernel_spmd

    g = {name: np.asarray(inputs[name])[0] for name in
         ("g_in", "g_mem", "g_cq", "g_ckv", "g_qa", "g_ka", "g_qm", "g_km", "g_qb", "g_kb")}
    columns = [g["g_in"].reshape(KC, P).T, g["g_mem"].reshape(KC, P).T, g["g_cq"].reshape(2, P).T,
               g["g_ckv"].reshape(1, P).T]
    columns += [np.tile(g[name], 2)[:, None] for name in ("g_qa", "g_ka", "g_qm", "g_km")]
    columns += [np.tile(g[name][None, :], (P, 1)) for name in ("g_qb", "g_kb")]
    arrays = {
        "x": np.ascontiguousarray(inputs["x"])[0], "xT": np.ascontiguousarray(np.asarray(inputs["x"])[0].T),
        "mem": np.ascontiguousarray(inputs["mem"])[0],
        "memT": np.ascontiguousarray(np.asarray(inputs["mem"])[0].T),
        **{name: np.ascontiguousarray(inputs[name])[0] for name in
           ("w_in", "w_uq", "w_ukv", "w_mk", "w_mv", "w_out")},
        "gains": np.ascontiguousarray(np.concatenate(columns, axis=1)),
        "tables": shape_tables(), "chunk_mask": chunk_mask(),
    }
    nc = bacc.Bacc("TRN2", target_bir_lowering=False, num_devices=1)
    args = [nc.dram_tensor(f"in_{name}", a.shape, mybir.dt.from_np(a.dtype), kind="ExternalInput").ap()
            for name, a in arrays.items()]
    args.append(nc.dram_tensor("out_y", (SEQ, DM), F32, kind="ExternalOutput").ap())
    build_layer(nc, *args)
    r = run_bass_kernel_spmd(nc, [{f"in_{name}": a for name, a in arrays.items()}], core_ids=[0])
    return r.results[0]["out_y"].reshape(1, SEQ, DM)


def shape_tables():
    import numpy as np

    f = np.float32
    n = ROPE // 2
    inv = f(1.0) / (f(10000.0) ** (np.arange(n, dtype=f) / f(n)))
    ang = np.arange(SEQ, dtype=f)[:, None] * inv[None, :]
    cos, sin = np.cos(ang), np.sin(ang)
    rope = np.concatenate([cos, cos, -sin, sin], axis=1).reshape(NT, P, 4 * n).transpose(1, 0, 2).reshape(P, -1)
    ones = np.ones((P, 3), f)
    ones[:, :2] = 0
    ones[:P // 2, 0] = 1
    ones[P // 2:, 1] = 1
    dist = -np.abs((SEQ - P + np.arange(P))[:, None] - np.arange(SEQ)[None, :]).astype(f)
    slopes = (f(2.0) ** (f(-8.0) * np.arange(1, AH + 1, dtype=f) / f(AH))) / f(A_SCALE)
    return np.ascontiguousarray(np.concatenate(
        [np.eye(P, dtype=f), rope, ones, dist, np.tile(slopes, (P, NT))], axis=1).astype(f))


def chunk_mask():
    import numpy as np

    first = (np.arange(SEQ) % P < P // 2).astype(np.float32)
    own = np.kron(np.eye(NT, dtype=np.float32), np.ones((1, P), np.float32))
    rows = np.stack([own * first, own * (1 - first) * np.float32(NEG)])
    return np.ascontiguousarray(np.tile(rows, (1, 1, BH)).astype(np.float32))
```
